# Optimizing a Trainium2 kernel written in Bass

```python
import numpy as np
import jax
import jax.numpy as jnp
from jax import lax
import math
import jax, jax.numpy as jnp

D_MODEL = 1024
BATCH = 1
SEQ = 512
DEPTH = 1

HEAD_DIM = 64
NSA_HEADS = D_MODEL // (2 * HEAD_DIM)
NSA_KV_GROUPS = max(1, NSA_HEADS // 4)
NSA_HPG = NSA_HEADS // NSA_KV_GROUPS
NSA_CMP_LEN = 32
NSA_CMP_STRIDE = 16
NSA_CMP_HID = 128
NSA_SEL_BLOCK = 64
NSA_SEL_TOP = 16
NSA_WINDOW = 512
NSA_Q_CHUNK = 64
MOBA_HEADS = D_MODEL // (2 * HEAD_DIM)
MOBA_BLOCK = 256
MOBA_TOP = 3
MOBA_Q_CHUNK = 32
N_EXPERTS = 32
TOP_K = 4
D_FF = 1024
SWIGLU_LIMIT = 7.0
SWIGLU_ALPHA = 1.702
MOE_BLOCK = 128
EPS = 1e-6
NEG = -1e30
FORCE_SCORE = 1e4

NSA_W = NSA_HEADS * HEAD_DIM
NSA_KV_W = NSA_KV_GROUPS * HEAD_DIM
MOBA_W = MOBA_HEADS * HEAD_DIM
MIX_W = NSA_W + MOBA_W
IN_WIDTHS = (NSA_W, NSA_KV_W, NSA_KV_W, NSA_KV_W, NSA_KV_W, NSA_KV_W, NSA_KV_W,
             3 * NSA_HEADS, MOBA_W, MOBA_W, MOBA_W)
IN_W = sum(IN_WIDTHS)


def rms_norm(x, g):
    xf = x.astype(jnp.float32)
    y = xf * lax.rsqrt(jnp.mean(xf * xf, axis=-1, keepdims=True) + EPS)
    return (y * g.astype(jnp.float32)).astype(x.dtype)

def alibi_slopes(n):
    return jnp.asarray(2.0 ** (-8.0 * np.arange(1, n + 1) / n), dtype=jnp.float32)

def masked_softmax(s, mask):
    s = jnp.where(mask, s.astype(jnp.float32), NEG)
    p = jax.nn.softmax(s, axis=-1)
    return jnp.where(mask, p, 0.0)

def _heads(t, n_heads):
    b, s, _ = t.shape
    return t.reshape(b, s, n_heads, HEAD_DIM).transpose(0, 2, 1, 3)

_gather_blocks = jax.vmap(jax.vmap(lambda blocks, idx: blocks[idx]))

def _compress(kv, pos, w1, w2):
    s = kv.shape[2]
    n_cmp = (s - NSA_CMP_LEN) // NSA_CMP_STRIDE + 1
    idx = NSA_CMP_STRIDE * np.arange(n_cmp)[:, None] + np.arange(NSA_CMP_LEN)[None, :]
    blocks = kv[:, :, idx] + pos
    flat = blocks.reshape(kv.shape[0], kv.shape[1], n_cmp, NSA_CMP_LEN * HEAD_DIM)
    return jax.nn.gelu(flat @ w1) @ w2

def nsa_mixer(q, k_cmp, v_cmp, k_slc, v_slc, k_win, v_win, gates, k_gain, cmp_pos, cmp_w1, cmp_w2):
    B, G, Hg, S, dh = q.shape
    scale = dh ** -0.5
    sl = alibi_slopes(G * Hg).reshape(1, G, Hg, 1, 1)
    kc = rms_norm(_compress(k_cmp, cmp_pos[0], cmp_w1[0], cmp_w2[0]), k_gain)
    vc = _compress(v_cmp, cmp_pos[1], cmp_w1[1], cmp_w2[1])
    n_cmp = kc.shape[2]
    cmp_start = NSA_CMP_STRIDE * np.arange(n_cmp)
    cmp_end = jnp.asarray(cmp_start + NSA_CMP_LEN - 1, dtype=jnp.int32)
    cmp_center = jnp.asarray(cmp_start + 0.5 * (NSA_CMP_LEN - 1), dtype=jnp.float32)
    n_sel = S // NSA_SEL_BLOCK
    sel_start = NSA_SEL_BLOCK * np.arange(n_sel)
    incid = jnp.asarray((cmp_start[:, None] <= sel_start[None, :] + NSA_SEL_BLOCK - 1)
                        & (cmp_start[:, None] + NSA_CMP_LEN - 1 >= sel_start[None, :]), dtype=jnp.float32)
    n_top = min(NSA_SEL_TOP, n_sel)
    ks = rms_norm(k_slc, k_gain).reshape(B, G, n_sel, NSA_SEL_BLOCK, dh)
    vs = v_slc.reshape(B, G, n_sel, NSA_SEL_BLOCK, dh)
    pad = ((0, 0), (0, 0), (NSA_WINDOW, 0), (0, 0))
    kw = jnp.pad(rms_norm(k_win, k_gain), pad)
    vw = jnp.pad(v_win, pad)
    blk_ids = jnp.arange(n_sel)[None, :]
    in_blk = jnp.arange(NSA_SEL_BLOCK)
    win_off = jnp.arange(NSA_WINDOW + NSA_Q_CHUNK)
    C = NSA_Q_CHUNK
    m_sel = n_top * NSA_SEL_BLOCK

    def chunk(q0):
        qc = lax.dynamic_slice_in_dim(q, q0, C, axis=3)
        gc = lax.dynamic_slice_in_dim(gates, q0, C, axis=3)
        t = q0 + jnp.arange(C)
        tf = t.astype(jnp.float32)
        s = jnp.einsum('bghcd,bgnd->bghcn', qc, kc, preferred_element_type=jnp.float32) * scale
        s = s - sl * (tf[:, None] - cmp_center[None, :])
        p_cmp = masked_softmax(s, cmp_end[None, :] <= t[:, None])
        o_cmp = jnp.einsum('bghcn,bgnd->bghcd', p_cmp.astype(vc.dtype), vc)
        imp = jnp.einsum('bghcn,nj->bgcj', p_cmp, incid)
        cur = (t // NSA_SEL_BLOCK)[:, None]
        forced = (blk_ids == 0) | (blk_ids == cur) | (blk_ids == cur - 1)
        imp = jnp.where(forced, FORCE_SCORE, imp)
        imp = jnp.where(blk_ids <= cur, imp, NEG)
        _, sel = lax.top_k(imp, n_top)
        ksel = _gather_blocks(ks, sel).reshape(B, G, C, m_sel, dh)
        vsel = _gather_blocks(vs, sel).reshape(B, G, C, m_sel, dh)
        pos = (sel[..., None] * NSA_SEL_BLOCK + in_blk).reshape(B, G, C, m_sel)
        dist = (t[None, None, :, None] - pos)[:, :, None]
        s = jnp.einsum('bghcd,bgcmd->bghcm', qc, ksel, preferred_element_type=jnp.float32) * scale
        s = s - sl * dist.astype(jnp.float32)
        p = masked_softmax(s, dist >= 0)
        o_sel = jnp.einsum('bghcm,bgcmd->bghcd', p.astype(vsel.dtype), vsel)
        kwc = lax.dynamic_slice_in_dim(kw, q0, NSA_WINDOW + C, axis=2)
        vwc = lax.dynamic_slice_in_dim(vw, q0, NSA_WINDOW + C, axis=2)
        pos_w = q0 - NSA_WINDOW + win_off
        dist_w = t[:, None] - pos_w[None, :]
        mask_w = (dist_w >= 0) & (dist_w < NSA_WINDOW) & (pos_w >= 0)[None, :]
        s = jnp.einsum('bghcd,bgkd->bghck', qc, kwc, preferred_element_type=jnp.float32) * scale
        s = s - sl * dist_w.astype(jnp.float32)
        p = masked_softmax(s, mask_w)
        o_win = jnp.einsum('bghck,bgkd->bghcd', p.astype(vwc.dtype), vwc)
        return gc[..., 0:1] * o_cmp + gc[..., 1:2] * o_sel + gc[..., 2:3] * o_win

    out = lax.map(chunk, jnp.arange(0, S, C))
    return out.transpose(1, 0, 4, 2, 3, 5).reshape(B, S, G * Hg * dh)

def moba_mixer(q, k, v):
    B, H, S, dh = q.shape
    scale = dh ** -0.5
    sl = alibi_slopes(H).reshape(1, H, 1, 1)
    n_blk = -(-S // MOBA_BLOCK)
    pad = ((0, 0), (0, 0), (0, n_blk * MOBA_BLOCK - S), (0, 0))
    kp = jnp.pad(k, pad)
    vp = jnp.pad(v, pad)
    kb = kp.reshape(B, H, n_blk, MOBA_BLOCK, dh)
    vb = vp.reshape(B, H, n_blk, MOBA_BLOCK, dh)
    kmean = jnp.mean(kb.astype(jnp.float32), axis=3)
    n_top = min(MOBA_TOP, n_blk - 1)
    in_blk = jnp.arange(MOBA_BLOCK)
    blk_ids = jnp.arange(n_blk)
    C = MOBA_Q_CHUNK
    m_g = n_top * MOBA_BLOCK

    def chunk(q0):
        qc = lax.dynamic_slice_in_dim(q, q0, C, axis=2)
        t = q0 + jnp.arange(C)
        cb = q0 // MOBA_BLOCK
        kcur = lax.dynamic_slice_in_dim(kp, cb * MOBA_BLOCK, MOBA_BLOCK, axis=2)
        vcur = lax.dynamic_slice_in_dim(vp, cb * MOBA_BLOCK, MOBA_BLOCK, axis=2)
        dist_c = t[:, None] - (cb * MOBA_BLOCK + in_blk)[None, :]
        s_c = jnp.einsum('bhcd,bhkd->bhck', qc, kcur, preferred_element_type=jnp.float32) * scale
        s_c = s_c - sl * dist_c.astype(jnp.float32)
        mask_c = jnp.broadcast_to(dist_c >= 0, s_c.shape)
        if n_top > 0:
            gate = jnp.einsum('bhcd,bhnd->bhcn', qc, kmean, preferred_element_type=jnp.float32)
            gate = jnp.where(blk_ids < cb, gate, NEG)
            _, sel = lax.top_k(gate, n_top)
            kg = _gather_blocks(kb, sel).reshape(B, H, C, m_g, dh)
            vg = _gather_blocks(vb, sel).reshape(B, H, C, m_g, dh)
            pos_g = (sel[..., None] * MOBA_BLOCK + in_blk).reshape(B, H, C, m_g)
            dist_g = t[None, None, :, None] - pos_g
            s_g = jnp.einsum('bhcd,bhcmd->bhcm', qc, kg, preferred_element_type=jnp.float32) * scale
            s_g = s_g - sl * dist_g.astype(jnp.float32)
            mask_g = jnp.repeat(sel < cb, MOBA_BLOCK, axis=-1)
            p = masked_softmax(jnp.concatenate([s_g, s_c], axis=-1),
                               jnp.concatenate([mask_g, mask_c], axis=-1))
            o = (jnp.einsum('bhcm,bhcmd->bhcd', p[..., :m_g].astype(vg.dtype), vg)
                 + jnp.einsum('bhck,bhkd->bhcd', p[..., m_g:].astype(vcur.dtype), vcur))
        else:
            p = masked_softmax(s_c, mask_c)
            o = jnp.einsum('bhck,bhkd->bhcd', p.astype(vcur.dtype), vcur)
        return o

    out = lax.map(chunk, jnp.arange(0, S, C))
    return out.transpose(1, 0, 3, 2, 4).reshape(B, S, H * dh)

def hybrid_mixer(h, w_in, w_out, nsa_q_gain, nsa_k_gain, cmp_pos, cmp_w1, cmp_w2, moba_q_gain, moba_k_gain):
    B, S, _ = h.shape
    z = h @ w_in
    points = [int(v) for v in np.cumsum(IN_WIDTHS)[:-1]]
    q_n, kc, vc, ks, vs, kw, vw, g_n, q_m, k_m, v_m = jnp.split(z, points, axis=-1)
    qn = rms_norm(_heads(q_n, NSA_HEADS), nsa_q_gain).reshape(B, NSA_KV_GROUPS, NSA_HPG, S, HEAD_DIM)
    gates = jax.nn.sigmoid(g_n.reshape(B, S, NSA_KV_GROUPS, NSA_HPG, 3)).transpose(0, 2, 3, 1, 4)
    o_nsa = nsa_mixer(qn, _heads(kc, NSA_KV_GROUPS), _heads(vc, NSA_KV_GROUPS),
                      _heads(ks, NSA_KV_GROUPS), _heads(vs, NSA_KV_GROUPS),
                      _heads(kw, NSA_KV_GROUPS), _heads(vw, NSA_KV_GROUPS),
                      gates, nsa_k_gain, cmp_pos, cmp_w1, cmp_w2)
    o_moba = moba_mixer(rms_norm(_heads(q_m, MOBA_HEADS), moba_q_gain),
                        rms_norm(_heads(k_m, MOBA_HEADS), moba_k_gain),
                        _heads(v_m, MOBA_HEADS))
    return jnp.concatenate([o_nsa, o_moba], axis=-1) @ w_out

def sparse_moe(h, router_w, router_b, w1, b1, w2, b2):
    B, S, D = h.shape
    T = B * S
    hf = h.reshape(T, D)
    logits = (hf @ router_w + router_b).astype(jnp.float32)
    top_val, top_idx = lax.top_k(logits, TOP_K)
    gate = jax.nn.softmax(top_val, axis=-1)
    A = T * TOP_K
    e_flat = top_idx.reshape(A)
    tok_flat = jnp.arange(A, dtype=jnp.int32) // TOP_K
    w_flat = gate.reshape(A).astype(h.dtype)
    order = jnp.argsort(e_flat)
    e_s, tok_s, w_s = e_flat[order], tok_flat[order], w_flat[order]
    counts = jnp.bincount(e_flat, length=N_EXPERTS)
    padded = (counts + MOE_BLOCK - 1) // MOE_BLOCK * MOE_BLOCK
    start = jnp.cumsum(counts) - counts
    pend = jnp.cumsum(padded)
    pstart = pend - padded
    dest = pstart[e_s] + jnp.arange(A) - start[e_s]
    R = A + N_EXPERTS * MOE_BLOCK
    n_blocks = R // MOE_BLOCK
    row_tok = jnp.zeros((R,), jnp.int32).at[dest].set(tok_s)
    row_w = jnp.zeros((R,), h.dtype).at[dest].set(w_s)
    blk_e = jnp.minimum(jnp.searchsorted(pend, jnp.arange(n_blocks) * MOE_BLOCK, side='right'), N_EXPERTS - 1)

    def expert_block(args):
        e, toks, wts = args
        u = hf[toks] @ w1[e] + b1[e]
        g_, lin = u[:, :D_FF], u[:, D_FF:]
        g_ = jnp.minimum(g_, SWIGLU_LIMIT)
        lin = jnp.clip(lin, -SWIGLU_LIMIT, SWIGLU_LIMIT)
        y = ((lin + 1.0) * g_ * jax.nn.sigmoid(SWIGLU_ALPHA * g_)) @ w2[e] + b2[e]
        return y * wts[:, None]

    y = lax.map(expert_block, (blk_e, row_tok.reshape(n_blocks, MOE_BLOCK), row_w.reshape(n_blocks, MOE_BLOCK)))
    out = jax.ops.segment_sum(y.reshape(R, D), row_tok, num_segments=T)
    return out.reshape(B, S, D)

def first_inputs(seed: int = 0) -> dict:
    key = jax.random.key(seed)
    ks = jax.random.split(key, 21)
    n = jax.random.normal
    f32 = jnp.float32
    D = D_MODEL
    return {
        'x': n(ks[0], (BATCH, SEQ, D), f32),
        'c': n(ks[1], (BATCH, D), f32),
        'ada_w': n(ks[2], (DEPTH, D, 6 * D), f32) * (0.5 * D ** -0.5),
        'ada_b': n(ks[3], (DEPTH, 6 * D), f32) * 0.01,
        'ln1_g': 1.0 + 0.01 * n(ks[4], (DEPTH, D), f32),
        'ln2_g': 1.0 + 0.01 * n(ks[5], (DEPTH, D), f32),
        'w_in': n(ks[6], (DEPTH, D, IN_W), f32) * D ** -0.5,
        'nsa_q_gain': 1.0 + 0.01 * n(ks[7], (DEPTH, HEAD_DIM), f32),
        'nsa_k_gain': 1.0 + 0.01 * n(ks[8], (DEPTH, HEAD_DIM), f32),
        'nsa_cmp_pos': 0.1 * n(ks[9], (DEPTH, 2, NSA_CMP_LEN, HEAD_DIM), f32),
        'nsa_cmp_w1': n(ks[10], (DEPTH, 2, NSA_CMP_LEN * HEAD_DIM, NSA_CMP_HID), f32) * (NSA_CMP_LEN * HEAD_DIM) ** -0.5,
        'nsa_cmp_w2': n(ks[11], (DEPTH, 2, NSA_CMP_HID, HEAD_DIM), f32) * NSA_CMP_HID ** -0.5,
        'moba_q_gain': 1.0 + 0.01 * n(ks[12], (DEPTH, HEAD_DIM), f32),
        'moba_k_gain': 1.0 + 0.01 * n(ks[13], (DEPTH, HEAD_DIM), f32),
        'w_out': n(ks[14], (DEPTH, MIX_W, D), f32) * MIX_W ** -0.5,
        'router_w': n(ks[15], (DEPTH, D, N_EXPERTS), f32) * D ** -0.5,
        'router_b': 0.01 * n(ks[16], (DEPTH, N_EXPERTS), f32),
        'exp_w1': n(ks[17], (DEPTH, N_EXPERTS, D, 2 * D_FF), f32) * D ** -0.5,
        'exp_b1': 0.01 * n(ks[18], (DEPTH, N_EXPERTS, 2 * D_FF), f32),
        'exp_w2': n(ks[19], (DEPTH, N_EXPERTS, D_FF, D), f32) * D_FF ** -0.5,
        'exp_b2': 0.01 * n(ks[20], (DEPTH, N_EXPERTS, D), f32),
    }

def first_block(x, c, ada_w, ada_b, ln1_g, ln2_g, w_in, nsa_q_gain, nsa_k_gain, nsa_cmp_pos, nsa_cmp_w1,
              nsa_cmp_w2, moba_q_gain, moba_k_gain, w_out, router_w, router_b, exp_w1, exp_b1, exp_w2, exp_b2):
    cond = jax.nn.silu(c)
    for l in range(DEPTH):
        mod = (cond @ ada_w[l] + ada_b[l])[:, None, :]
        sh1, sc1, g1, sh2, sc2, g2 = jnp.split(mod, 6, axis=-1)
        h = rms_norm(x, ln1_g[l]) * (1.0 + sc1) + sh1
        x = x + g1 * hybrid_mixer(h, w_in[l], w_out[l], nsa_q_gain[l], nsa_k_gain[l], nsa_cmp_pos[l],
                                  nsa_cmp_w1[l], nsa_cmp_w2[l], moba_q_gain[l], moba_k_gain[l])
        h = rms_norm(x, ln2_g[l]) * (1.0 + sc2) + sh2
        x = x + g2 * sparse_moe(h, router_w[l], router_b[l], exp_w1[l], exp_b1[l], exp_w2[l], exp_b2[l])
    return x


CONV_C = 1024
CONV_W = 31
FOX_HEADS = 16
FOX_HD = 64
FOX_W = FOX_HEADS * FOX_HD
Q_BLOCK = 128
IN_SPLITS = (CONV_C, CONV_C, FOX_W, FOX_W, FOX_W, FOX_HEADS, D_MODEL, D_MODEL)
IN_COLS = sum(IN_SPLITS)
PEER_HEADS = 8
PEER_NKEYS = 128
PEER_EXPERTS = PEER_NKEYS * PEER_NKEYS
PEER_DK = 256
PEER_TOPK = 16
PEER_CHUNK = 128
NEG_2 = -1e30


def rmsnorm(x, g):
    xf = x.astype(jnp.float32)
    y = xf * lax.rsqrt(jnp.mean(xf * xf, axis=-1, keepdims=True) + EPS)
    return (y * g.astype(jnp.float32)).astype(x.dtype)

def layernorm(x, g, b):
    xf = x.astype(jnp.float32)
    mu = jnp.mean(xf, axis=-1, keepdims=True)
    var = jnp.mean(jnp.square(xf - mu), axis=-1, keepdims=True)
    y = (xf - mu) * lax.rsqrt(var + EPS)
    return (y * g.astype(jnp.float32) + b.astype(jnp.float32)).astype(x.dtype)

def conformer_conv(z_val, z_gate, conv_w, conv_b, ln_g, ln_b, w_conv_out):
    z = z_val * jax.nn.sigmoid(z_gate)
    z = lax.conv_general_dilated(
        z, conv_w[:, None, :].astype(z.dtype), window_strides=(1,),
        padding=[(CONV_W - 1, 0)], dimension_numbers=("NWC", "WIO", "NWC"),
        feature_group_count=CONV_C) + conv_b
    z = layernorm(z, ln_g, ln_b)
    z = z * jax.nn.sigmoid(z)
    return z @ w_conv_out

def forgetting_attention(q, k, v, c):
    B, H, S, hd = q.shape
    nb = S // Q_BLOCK
    scale = 1.0 / math.sqrt(hd)
    qb = q.reshape(B, H, nb, Q_BLOCK, hd).transpose(2, 0, 1, 3, 4)
    cb = c.reshape(B, H, nb, Q_BLOCK).transpose(2, 0, 1, 3)
    kf = k.astype(jnp.float32)
    vf = v.astype(jnp.float32)
    kpos = jnp.arange(S)

    def one_block(args):
        qi, ci, i = args
        s = jnp.einsum("bhqd,bhkd->bhqk", qi.astype(jnp.float32), kf) * scale
        s = s + ci[..., :, None] - c[:, :, None, :]
        qpos = i * Q_BLOCK + jnp.arange(Q_BLOCK)
        mask = kpos[None, :] <= qpos[:, None]
        p = jax.nn.softmax(jnp.where(mask, s, NEG_2), axis=-1)
        return jnp.einsum("bhqk,bhkd->bhqd", p, vf)

    out = lax.map(one_block, (qb, cb, jnp.arange(nb)))
    return out.transpose(1, 2, 0, 3, 4).reshape(B, H, S, hd).astype(q.dtype)

def peer_ffn(h, peer_wq, peer_k1, peer_k2, peer_u, peer_v):
    B, S, D = h.shape
    T = B * S
    ht = h.reshape(T, D)
    q = (ht @ peer_wq).reshape(T, PEER_HEADS, PEER_DK).astype(jnp.float32)
    half = PEER_DK // 2
    s1 = jnp.einsum("thd,hnd->thn", q[..., :half], peer_k1.astype(jnp.float32))
    s2 = jnp.einsum("thd,hnd->thn", q[..., half:], peer_k2.astype(jnp.float32))
    v1, i1 = lax.top_k(s1, PEER_TOPK)
    v2, i2 = lax.top_k(s2, PEER_TOPK)
    cand = (v1[..., :, None] + v2[..., None, :]).reshape(T, PEER_HEADS, PEER_TOPK * PEER_TOPK)
    sc, pos = lax.top_k(cand, PEER_TOPK)
    e1 = jnp.take_along_axis(i1, pos // PEER_TOPK, axis=-1)
    e2 = jnp.take_along_axis(i2, pos % PEER_TOPK, axis=-1)
    experts = (e1 * PEER_NKEYS + e2).reshape(T, PEER_HEADS * PEER_TOPK)
    gates = jax.nn.softmax(sc, axis=-1).reshape(T, PEER_HEADS * PEER_TOPK)
    nc = T // PEER_CHUNK

    def chunk(args):
        hc, ec, gc = args
        u = peer_u[ec]
        a = jax.nn.gelu(jnp.einsum("ckd,cd->ck", u, hc).astype(jnp.float32)) * gc
        vv = peer_v[ec]
        return jnp.einsum("ck,ckd->cd", a.astype(vv.dtype), vv)

    out = lax.map(chunk, (ht.reshape(nc, PEER_CHUNK, D),
                          experts.reshape(nc, PEER_CHUNK, -1),
                          gates.reshape(nc, PEER_CHUNK, -1)))
    return out.reshape(B, S, D).astype(h.dtype)

def second_inputs(seed: int = 0) -> dict:
    key = jax.random.key(seed)
    ks = jax.random.split(key, 20)
    f32 = jnp.float32
    D = D_MODEL
    nrm = lambda k, shape, s: jax.random.normal(k, shape, f32) * s
    return {
        "x": nrm(ks[0], (BATCH, SEQ, D), 1.0),
        "norm1_g": 1.0 + nrm(ks[1], (D,), 0.02),
        "w_in": nrm(ks[2], (D, IN_COLS), D ** -0.5),
        "conv_w": nrm(ks[3], (CONV_W, CONV_C), CONV_W ** -0.5),
        "conv_b": nrm(ks[4], (CONV_C,), 0.02),
        "conv_ln_g": 1.0 + nrm(ks[5], (CONV_C,), 0.02),
        "conv_ln_b": nrm(ks[6], (CONV_C,), 0.02),
        "w_conv_out": nrm(ks[7], (CONV_C, D), CONV_C ** -0.5),
        "fox_bf": 1.0 + 4.0 * jax.random.uniform(ks[8], (FOX_HEADS,), f32),
        "w_fox_out": nrm(ks[9], (FOX_W, D), FOX_W ** -0.5),
        "w_out": nrm(ks[10], (D, D), D ** -0.5),
        "norm2_g": 1.0 + nrm(ks[11], (D,), 0.02),
        "peer_wq": nrm(ks[12], (D, PEER_HEADS * PEER_DK), D ** -0.5),
        "peer_k1": nrm(ks[13], (PEER_HEADS, PEER_NKEYS, PEER_DK // 2), (PEER_DK // 2) ** -0.5),
        "peer_k2": nrm(ks[14], (PEER_HEADS, PEER_NKEYS, PEER_DK // 2), (PEER_DK // 2) ** -0.5),
        "peer_u": nrm(ks[15], (PEER_EXPERTS, D), D ** -0.5),
        "peer_v": nrm(ks[16], (PEER_EXPERTS, D), PEER_HEADS ** -0.5),
        "normf_g": 1.0 + nrm(ks[17], (D,), 0.02),
    }

def second_block(x, norm1_g, w_in, conv_w, conv_b, conv_ln_g, conv_ln_b, w_conv_out,
              fox_bf, w_fox_out, w_out, norm2_g, peer_wq, peer_k1, peer_k2,
              peer_u, peer_v, normf_g):
    B, S, D = x.shape
    idx = np.cumsum(IN_SPLITS)[:-1].tolist()
    for _ in range(DEPTH):
        h = rmsnorm(x, norm1_g)
        z = h @ w_in
        a_val, a_gate, q, k, v, f_logit, g_a, g_b = jnp.split(z, idx, axis=-1)
        ya = conformer_conv(a_val, a_gate, conv_w, conv_b, conv_ln_g, conv_ln_b, w_conv_out)
        heads = lambda t: t.reshape(B, S, FOX_HEADS, FOX_HD).transpose(0, 2, 1, 3)
        log_f = jax.nn.log_sigmoid(f_logit.astype(jnp.float32) + fox_bf.astype(jnp.float32))
        c = jnp.cumsum(log_f, axis=1).transpose(0, 2, 1)
        ob = forgetting_attention(heads(q), heads(k), heads(v), c)
        yb = ob.transpose(0, 2, 1, 3).reshape(B, S, FOX_W) @ w_fox_out
        mix = (jax.nn.sigmoid(g_a) * ya + jax.nn.sigmoid(g_b) * yb) @ w_out
        x = x + mix
        x = x + peer_ffn(rmsnorm(x, norm2_g), peer_wq, peer_k1, peer_k2, peer_u, peer_v)
    return rmsnorm(x, normf_g)


def setup_inputs(seed=0):
    out = dict(first_inputs(seed))
    for name, value in second_inputs(seed + 1).items():
        if name != "x":
            out[name + "_2"] = value
    return out


def reference(
    x, c, ada_w, ada_b, ln1_g, ln2_g, w_in, nsa_q_gain, nsa_k_gain, nsa_cmp_pos, nsa_cmp_w1,
    nsa_cmp_w2, moba_q_gain, moba_k_gain, w_out, router_w, router_b, exp_w1, exp_b1, exp_w2,
    exp_b2, norm1_g_2, w_in_2, conv_w_2, conv_b_2, conv_ln_g_2, conv_ln_b_2, w_conv_out_2,
    fox_bf_2, w_fox_out_2, w_out_2, norm2_g_2, peer_wq_2, peer_k1_2, peer_k2_2, peer_u_2,
    peer_v_2, normf_g_2,
):
    x = first_block(
        x, c, ada_w, ada_b, ln1_g, ln2_g, w_in, nsa_q_gain, nsa_k_gain, nsa_cmp_pos, nsa_cmp_w1,
        nsa_cmp_w2, moba_q_gain, moba_k_gain, w_out, router_w, router_b, exp_w1, exp_b1, exp_w2,
        exp_b2,
    )
    return second_block(
        x, norm1_g_2, w_in_2, conv_w_2, conv_b_2, conv_ln_g_2, conv_ln_b_2, w_conv_out_2,
        fox_bf_2, w_fox_out_2, w_out_2, norm2_g_2, peer_wq_2, peer_k1_2, peer_k2_2, peer_u_2,
        peer_v_2, normf_g_2,
    )


_drawn_inputs = setup_inputs


def setup_inputs(seed=0):
    import zlib

    import numpy as np

    out = dict(_drawn_inputs(seed))
    spreads = {}
    factors = {'ln1_g': 7.255,
     'ln2_g': 2.974,
     'nsa_q_gain': 8.0,
     'nsa_k_gain': 8.0,
     'moba_q_gain': 8.0,
     'moba_k_gain': 8.0,
     'router_b': 3.07,
     'exp_b1': 7.301,
     'exp_b2': 34.404,
     'norm1_g_2': 3.031,
     'conv_ln_g_2': 19.917,
     'conv_ln_b_2': 21.136,
     'normf_g_2': 8.233,
     'conv_b_2': 8.0,
     'norm2_g_2': 7.295}
    for name, (base, spread) in spreads.items():
        noise = np.random.default_rng([zlib.crc32(name.encode()), seed]).standard_normal(out[name].shape)
        drawn = base * np.exp(spread * noise) if base else spread * noise
        out[name] = jnp.asarray(drawn.astype(out[name].dtype))
    for name, factor in factors.items():
        out[name] = (out[name] * factor).astype(out[name].dtype)
    return out
```

```python
from contextlib import ExitStack

import concourse.bass as bass
from concourse import mybir

F32 = mybir.dt.float32
F32R = mybir.dt.float32r
BF16 = mybir.dt.bfloat16
U32 = mybir.dt.uint32
I32 = mybir.dt.int32
ALU = mybir.AluOpType
ACT = mybir.ActivationFunctionType
AX = mybir.AxisListType.X

P = 128
D = 1024
S = 512
NT = S // P
KC = D // P
HD = 64
AUG = HD + 2
EPS = 1e-6
NEG = -1e30
W = 512
SLOTS = 4

NSA_HEADS, MOBA_HEADS, GROUPS = 8, 8, 2
N_CMP = (S - 32) // 16 + 1
CMP_LEN, CMP_STRIDE, CMP_HID = 32, 16, 128
C_QN, C_KC, C_VC, C_KS, C_VS, C_KW, C_VW, C_G, C_QM, C_KM, C_VM = (
    0, 512, 640, 768, 896, 1024, 1152, 1280, 1304, 1816, 2328)
IN1 = 2840
N_EXP, TOP_K, FF = 32, 4, 1024
MAX_BLOCKS = (S * TOP_K + N_EXP * (P - 1)) // P

CONV_W = 31
FOX_HEADS = 16
PEER_HEADS, PEER_TOPK, PEER_KEYS = 8, 16, 128

CONST_COLS = {}


def lay_constants():
    import numpy as np
    p = np.arange(P)[:, None].astype(np.float32)
    j = np.arange(P)[None, :].astype(np.float32)
    t = (np.arange(NT)[None, :] * P + p).astype(np.float32)
    slopes = 2.0 ** (-np.arange(1, 9, dtype=np.float32))
    parts = {
        "ident": (p == j),
        "causal": np.where(j <= p, 0.0, NEG),
        "cum_incl": (p <= j),
        "cum_excl": (p < j),
        "ones": np.ones((P, P)),
        "aug_q": np.stack([-slopes[None, :, None] * t[:, None, :],
                           np.broadcast_to(slopes[None, :, None], (P, 8, NT))], -1),
        "aug_k": np.stack([np.ones((P, NT)), t], -1),
        "aug_c": np.stack([np.ones((P, 1)), p * CMP_STRIDE + 0.5 * (CMP_LEN - 1)], -1),
        "cmp_mask": np.where(np.arange(N_CMP)[None, None, :] * CMP_STRIDE + CMP_LEN - 1 <= t[:, :, None], 0.0, NEG),
        "cmp_any": (t >= CMP_LEN - 1),
        "iota": np.broadcast_to(np.arange(48, dtype=np.float32)[None, :], (P, 48)),
        "expert_of_row": p % N_EXP,
        "tok": t,
    }
    at, cols = 0, []
    for name, a in parts.items():
        a = np.asarray(a, np.float32).reshape(P, -1)
        CONST_COLS[name] = (at, a.shape[1])
        at += a.shape[1]
        cols.append(a)
    return np.ascontiguousarray(np.concatenate(cols, 1))


class Chain:

    def __init__(self, eng, sem):
        self.eng, self.sem, self.n, self.base = eng, sem, 0, 0

    def __call__(self, ins):
        self.n += 1
        ins.then_inc(self.sem, 1)
        self.eng.wait_ge(self.sem, self.base + self.n)

    def loop(self, i, per):
        self.start, self.per = self.n, per
        self.base, self.n = i * per + self.start, 0

    def end(self, count):
        assert self.n == self.per, (self.n, self.per)
        self.n, self.base = self.start + count * self.per, 0


class Env:

    def __init__(self, nc, ctx, d):
        self.nc, self.d = nc, d
        self.x = ctx.enter_context(nc.sbuf_tensor("x_res", [P, NT, D], F32))
        self.ring = ctx.enter_context(nc.sbuf_tensor("ring", [P, 2 * SLOTS, 2048], F32))
        n = sum(c for _, c in CONST_COLS.values())
        self.consts = ctx.enter_context(nc.sbuf_tensor("consts_sb", [P, n], F32))
        self.w_landed = [ctx.enter_context(nc.semaphore(f"w_landed{i}")) for i in range(SLOTS)]
        self.w_used = ctx.enter_context(nc.semaphore("w_used"))
        self.loaded = self.used = 0

    def const(self, name, rows=P):
        at, n = CONST_COLS[name]
        return self.consts[0:rows, at:at + n]

    def slot(self, i):
        i %= SLOTS
        return self.ring[:, 2 * i:2 * i + 2, :].rearrange("p a b -> p (a b)").rearrange("p (k n) -> p k n", k=KC)

    def load(self, sp, w, c0, cols):
        if self.loaded >= SLOTS:
            sp.wait_ge(self.w_used, self.loaded - SLOTS + 1)
        sp.dma_start(self.slot(self.loaded)[:, :, 0:cols],
                     w.rearrange("(k p) n -> p k n", p=P)[:, :, c0:c0 + cols]
                     ).then_inc(self.w_landed[self.loaded % SLOTS], 16)
        self.loaded += 1

    def arrived(self, pe):
        i = self.used
        self.used += 1
        pe.wait_ge(self.w_landed[i % SLOTS], 16 * (i // SLOTS + 1))
        return self.slot(i)


def stage(nc, name):
    ctx = ExitStack()
    sb = lambda n, shape, dt=F32: ctx.enter_context(nc.sbuf_tensor(f"{name}_{n}", shape, dt))
    ps = lambda n, shape, dt=F32: ctx.enter_context(nc.psum_tensor(f"{name}_{n}", shape, dt))
    sems = []

    def sem(n):
        sems.append(nc.alloc_semaphore(f"{name}_{n}"))
        return sems[-1]

    def zero():
        if sems:
            nc.clear_and_free_semaphores(sems)
            nc.all_engine_barrier()

    ctx.callback(zero)
    return ctx, sb, ps, sem


def modulation(env, mod):
    nc, d = env.nc, env.d
    ctx, sb, ps, sem = stage(nc, "ada")
    with ctx:
        c_col = sb("c_col", [P, KC]); c_act = sb("c_act", [P, KC]); c_rows = sb("c_rows", [P, KC, P])
        g_row = sb("g_row", [P, 2, D])
        acc = ps("acc", [P, 4, W])
        c_landed, landed, cond, rows, added, chain_s = (sem(n) for n in (
            "c_landed", "landed", "cond", "rows", "added", "chain"))
        block = ctx.enter_context(nc.Block())
        tiles = 6 * D // W

        @block.sync
        def _(sp):
            sp.dma_start(c_col[:], d["c_col"]).then_inc(c_landed, 16)
            sp.dma_start(env.consts[:], d["consts"]).then_inc(landed, 16)
            for j in range(SLOTS):
                env.load(sp, d["ada_w"], j * W, W)
            sp.dma_start(mod[:], d["ada_b"].partition_broadcast(P)).then_inc(landed, 16)
            sp.dma_start(g_row[:, 0, :], d["ln1_g"].partition_broadcast(P)).then_inc(landed, 16)
            sp.dma_start(g_row[:, 1, :], d["ln2_g"].partition_broadcast(P)).then_inc(landed, 16)
            sp.dma_start(env.x[:], d["x"].rearrange("(t p) n -> p t n", p=P)).then_inc(landed, 16)
            for j in range(SLOTS, tiles):
                env.load(sp, d["ada_w"], j * W, W)
            for j in range(SLOTS):
                env.load(sp, d["w_in"], j * W, W)

        @block.scalar
        def _(act):
            act.wait_ge(c_landed, 16)
            nc.scalar.activation(c_act[:], c_col[:], ACT.Silu).then_inc(cond, 1)

        @block.tensor
        def _(pe):
            pe.wait_ge(rows, 1)
            for j in range(tiles):
                w = env.arrived(pe)
                if j >= 4:
                    pe.wait_ge(added, j - 3)
                for k in range(KC):
                    last = nc.tensor.matmul(acc[:, j % 4, :], c_rows[:, k, :], w[:, k, :],
                                            start=(k == 0), stop=(k == KC - 1))
                last.then_inc(env.w_used, 1)

        @block.vector
        def _(dve):
            chain = Chain(dve, chain_s)
            dve.wait_ge(cond, 1)
            nc.vector.tensor_copy(c_rows[:], c_act[:].unsqueeze(2).to_broadcast([P, KC, P])).then_inc(rows, 1)
            dve.wait_ge(landed, 80)
            for j in range(tiles):
                dve.wait_ge(env.w_used, j + 1)
                cut = mod[:, j * W:(j + 1) * W]
                nc.vector.tensor_tensor(cut, acc[:, j % 4, :], cut, ALU.add).then_inc(added, 1)
            dve.wait_ge(added, tiles)
            for i, part in enumerate((1, 4)):
                cut = mod[:, part * D:(part + 1) * D]
                chain(nc.vector.scalar_tensor_tensor(cut, cut, 1.0, g_row[:, i, :], ALU.add, ALU.mult))


def norm_transpose(env, name, scale_row, shift_row, ht, h=None, h_dram=None, gain=None, prefetch=()):
    nc = env.nc
    ctx, sb, ps, sem = stage(nc, name)
    with ctx:
        if h is None:
            h = sb("h", [P, NT, D])
        if gain is not None:
            scale_row = sb("gain_row", [P, D])[:]
        junk = sb("junk", [P, D]); ms = sb("ms", [P, NT]); rstd = sb("rstd", [P, NT]); eps = sb("eps", [P, 1])
        turned = ps("turned", [P, 4, W])
        landed, eps_set, root, ready, turn, act_chain, chain_s, stored = (sem(n) for n in (
            "landed", "eps_set", "root", "ready", "turn", "act_chain", "chain", "stored"))
        moved = [sem("moved_by_act"), sem("moved_by_dve")]
        block = ctx.enter_context(nc.Block())
        half = KC // 4

        @block.sync
        def _(sp):
            if gain is not None:
                sp.dma_start(scale_row, gain.partition_broadcast(P)).then_inc(landed, 16)
            for w, c0, cols in prefetch:
                env.load(sp, w, c0, cols)
            if h_dram is not None:
                sp.wait_ge(ready, NT)
                sp.dma_start(h_dram.rearrange("(t p) n -> p t n", p=P), h[:]).then_inc(stored, 16)
                sp.wait_ge(stored, 16)

        @block.scalar
        def _(act):
            chain = Chain(act, act_chain)
            for t in range(NT):
                chain(nc.scalar.activation(junk[:], env.x[:, t, :], ACT.Square, accum_out=ms[:, t:t + 1]))
            act.wait_ge(eps_set, 1)
            nc.scalar.activation(rstd[:], ms[:], ACT.Sqrt, bias=eps[:], scale=1.0 / D).then_inc(root, 1)
            for n in range(0, NT * half, 2):
                act.wait_ge(turn, n + 1)
                t, q = n // half, n % half
                nc.scalar.copy(ht[:, 4 * q:4 * q + 4, t * P:(t + 1) * P],
                               turned[:, n % 4, :].rearrange("p (k c) -> p k c", k=4)).then_inc(moved[0], 1)

        @block.vector
        def _(dve):
            chain = Chain(dve, chain_s)
            nc.vector.memset(eps[:], EPS).then_inc(eps_set, 1)
            dve.wait_ge(root, 1)
            chain(nc.vector.reciprocal(rstd[:], rstd[:]))
            if gain is not None:
                dve.wait_ge(landed, 16)
            for t in range(NT):
                ins = nc.vector.scalar_tensor_tensor(h[:, t, :], env.x[:, t, :], rstd[:, t:t + 1], scale_row,
                                                     ALU.mult, ALU.mult)
                if shift_row is not None:
                    chain(ins)
                    ins = nc.vector.tensor_tensor(h[:, t, :], h[:, t, :], shift_row, ALU.add)
                ins.then_inc(ready, 1)
            for n in range(1, NT * half, 2):
                dve.wait_ge(turn, n + 1)
                t, q = n // half, n % half
                nc.vector.tensor_copy(ht[:, 4 * q:4 * q + 4, t * P:(t + 1) * P],
                                      turned[:, n % 4, :].rearrange("p (k c) -> p k c", k=4)).then_inc(moved[1], 1)

        @block.tensor
        def _(pe):
            for n in range(NT * half):
                t, q = n // half, n % half
                if q == 0:
                    pe.wait_ge(ready, t + 1)
                if n >= 4:
                    pe.wait_ge(moved[n % 2], n // 2 - 1)
                for i in range(4):
                    last = nc.tensor.transpose(turned[:, n % 4, i * P:(i + 1) * P],
                                               h[:, t, (4 * q + i) * P:(4 * q + i + 1) * P], env.const("ident"))
                last.then_inc(turn, 1)


def project(env, pe, acc, ht, tiles, freed, first=0):
    nc = env.nc
    for j, cols in enumerate(tiles):
        w = env.arrived(pe)
        if j + first >= 2:
            pe.wait_ge(freed, j + first - 1)
        for t in range(NT):
            for k in range(KC):
                last = nc.tensor.matmul(acc[:, (j + first) % 2, t, 0:cols], ht[:, k, t * P:(t + 1) * P], w[:, k, 0:cols],
                                        start=(k == 0), stop=(k == KC - 1))
        last.then_inc(env.w_used, 1)


def in_projection(env, ht, z):
    nc, d = env.nc, env.d
    ctx, sb, ps, sem = stage(nc, "in1")
    with ctx:
        gains = sb("gains", [P, 4, HD]); sq = sb("sq", [P, 8 * HD]); ms = sb("ms", [P, NT, 28]); eps = sb("eps", [P, 1])
        acc = ps("acc", [P, 2, NT, W])
        landed, freed, chain_s, act_s, summed, root, eps_set = (sem(n) for n in (
            "landed", "freed", "chain", "act_chain", "summed", "root", "eps_set"))
        block = ctx.enter_context(nc.Block())
        cols = [min(W, IN1 - c) for c in range(0, IN1, W)]
        base = env.used
        parts = ((C_QN, 8, 0), (C_KS, 2, 1), (C_KW, 2, 1), (C_QM, 8, 2), (C_KM, 8, 3))

        @block.sync
        def _(sp):
            for i, name in enumerate(("nsa_q_gain", "nsa_k_gain", "moba_q_gain", "moba_k_gain")):
                sp.dma_start(gains[:, i, :], d[name].partition_broadcast(P)).then_inc(landed, 16)
            for j in range(SLOTS, len(cols)):
                env.load(sp, d["w_in"], j * W, cols[j])

        @block.tensor
        def _(pe):
            project(env, pe, acc, ht, cols, freed)

        @block.scalar
        def _(act):
            for j, n in enumerate(cols):
                act.wait_ge(env.w_used, base + j + 1)
                nc.scalar.copy(z[:, :, j * W:j * W + n], acc[:, j % 2, :, 0:n]).then_inc(freed, 1)
            act.wait_ge(summed, 1)
            act.wait_ge(eps_set, 1)
            nc.scalar.activation(ms[:], ms[:], ACT.Sqrt, bias=eps[:], scale=1.0 / HD).then_inc(root, 1)

        @block.vector
        def _(dve):
            chain = Chain(dve, chain_s)
            nc.vector.memset(eps[:], EPS).then_inc(eps_set, 1)
            dve.wait_ge(landed, 64)
            for g in (0, 2):
                chain(nc.vector.tensor_scalar(gains[:, g, :], gains[:, g, :], HD ** -0.5, None, ALU.mult))
            at = 0
            for c0, heads, g in parts:
                dve.wait_ge(freed, (c0 + heads * HD - 1) // W + 1)
                for t in range(NT):
                    cut = z[:, t, c0:c0 + heads * HD]
                    chain(nc.vector.tensor_tensor(sq[:, 0:heads * HD], cut, cut, ALU.mult))
                    chain(nc.vector.tensor_reduce(ms[:, t, at:at + heads], sq[:, 0:heads * HD].rearrange("p (h e) -> p h e", e=HD), AX, ALU.add))
                at += heads
            dve.sem_inc(summed, 1)
            dve.wait_ge(root, 1)
            chain(nc.vector.reciprocal(ms[:], ms[:]))
            at = 0
            for c0, heads, g in parts:
                for t in range(NT):
                    cut = z[:, t, c0:c0 + heads * HD].rearrange("p (h e) -> p h e", e=HD)
                    chain(nc.vector.tensor_tensor(cut, cut, ms[:, t, at:at + heads].unsqueeze(2).to_broadcast([P, heads, HD]), ALU.mult))
                    chain(nc.vector.tensor_tensor(cut, cut, gains[:, g, :].unsqueeze(1).to_broadcast([P, heads, HD]), ALU.mult))
                at += heads


def compress(env, z, kct, vc):
    nc, d = env.nc, env.d
    ctx, sb, ps, sem = stage(nc, "cmp")
    with ctx:
        w1 = env.spare[:].rearrange("p (c l m) -> p c l m", c=2, l=CMP_LEN)
        w2 = sb("w2", [P, 2, HD]); pos = sb("pos", [P, 2, CMP_LEN]); gain = sb("gain", [P, HD])
        kvt = sb("kvt", [P, 2, S]); hid = sb("hid", [P, 2, GROUPS * N_CMP]); bias = sb("bias", [P, 2])
        kc = sb("kc", [P, GROUPS, AUG]); sq = sb("sq", [P, HD]); ms = sb("ms", [P, GROUPS]); eps = sb("eps", [P, 1])
        turned = ps("turned", [P, 2, S]); hps = ps("hps", [P, 4, W]); pps = ps("pps", [P, 2])
        ops = turned[:, 0, 0:2 * GROUPS * HD].rearrange("p (c g e) -> p c g e", c=2, g=GROUPS)
        kps = turned[:, 1, 0:GROUPS * N_CMP].rearrange("p (g n) -> p g n", g=GROUPS)
        landed, turn, moved, poss, bias_ok, hidden, gelu, out, eps_set, msum, root, normed, kturn, chain_s = (sem(n) for n in (
            "landed", "turn", "moved", "poss", "bias_ok", "hidden", "gelu", "out", "eps_set", "msum", "root", "normed", "kturn", "chain"))
        block = ctx.enter_context(nc.Block())

        @block.sync
        def _(sp):
            for half in range(2):
                rows = slice(half * HD, (half + 1) * HD)
                for c in range(2):
                    sp.dma_start(w1[rows, c], d["cmp_w1"][c].rearrange("(l e) m -> e l m", e=HD)).then_inc(landed, 16)
                sp.dma_start(pos[rows], d["cmp_pos"].rearrange("e (c l) -> e c l", c=2)).then_inc(landed, 16)
            sp.dma_start(w2[:], d["cmp_w2"].rearrange("c m e -> m c e")).then_inc(landed, 16)
            sp.dma_start(gain[:], d["nsa_k_gain"].partition_broadcast(P)).then_inc(landed, 16)
            for j in range(2):
                env.load(sp, d["w_out"], j * W, W)

        @block.tensor
        def _(pe):
            for c, c0 in enumerate((C_KC, C_VC)):
                for t in range(NT):
                    last = nc.tensor.transpose(turned[:, c, t * P:(t + 1) * P], z[:, t, c0:c0 + P], env.const("ident"))
                last.then_inc(turn, 1)
            pe.wait_ge(landed, 128)
            for c in range(2):
                for l in range(CMP_LEN):
                    last = nc.tensor.matmul(pps[:, c:c + 1], w1[0:HD, c, l, :], pos[0:HD, c, l:l + 1],
                                            start=(l == 0), stop=(l == CMP_LEN - 1))
                last.then_inc(poss, 1)
            for c in range(2):
                pe.wait_ge(moved, c + 1)
                for g in range(GROUPS):
                    rows = slice(g * HD, (g + 1) * HD)
                    for l in range(CMP_LEN):
                        last = nc.tensor.matmul(hps[:, 2 * c + g, 0:N_CMP], w1[rows, c, l, :],
                                                kvt[rows, c, l:l + CMP_STRIDE * (N_CMP - 1) + 1:CMP_STRIDE],
                                                start=(l == 0), stop=(l == CMP_LEN - 1))
                last.then_inc(hidden, 1)
            for c in range(2):
                pe.wait_ge(gelu, GROUPS * (c + 1))
                for g in range(GROUPS):
                    last = nc.tensor.matmul(ops[0:N_CMP, c, g, :], hid[:, c, g * N_CMP:(g + 1) * N_CMP], w2[:, c, :],
                                            start=True, stop=True)
                last.then_inc(out, 1)
            pe.wait_ge(normed, 1)
            for g in range(GROUPS):
                last = nc.tensor.transpose(kps[0:AUG, g, :], kc[0:N_CMP, g, :], env.const("ident")[0:N_CMP, 0:N_CMP])
            last.then_inc(kturn, 1)

        @block.scalar
        def _(act):
            for c in range(2):
                act.wait_ge(turn, c + 1)
                nc.scalar.copy(kvt[:, c, :], turned[:, c, :]).then_inc(moved, 1)
            act.wait_ge(bias_ok, 1)
            for c in range(2):
                act.wait_ge(hidden, c + 1)
                for g in range(GROUPS):
                    nc.scalar.activation(hid[:, c, g * N_CMP:(g + 1) * N_CMP], hps[:, 2 * c + g, 0:N_CMP],
                                         ACT.Gelu_apprx_tanh, bias=bias[:, c:c + 1]).then_inc(gelu, 1)
            act.wait_ge(msum, 1)
            nc.scalar.activation(ms[0:N_CMP], ms[0:N_CMP], ACT.Sqrt, bias=eps[0:N_CMP], scale=1.0 / HD).then_inc(root, 1)

        @block.vector
        def _(dve):
            chain = Chain(dve, chain_s)
            chain(nc.vector.memset(eps[:], EPS))
            dve.wait_ge(poss, 2)
            nc.vector.tensor_copy(bias[:], pps[:]).then_inc(bias_ok, 1)
            dve.wait_ge(out, 2)
            for g in range(GROUPS):
                chain(nc.vector.tensor_copy(kc[0:N_CMP, g, 0:HD], ops[0:N_CMP, 0, g, :]))
                chain(nc.vector.tensor_copy(kc[0:N_CMP, g, HD:AUG], env.const("aug_c", N_CMP)))
                chain(nc.vector.tensor_copy(vc[0:N_CMP, g, :], ops[0:N_CMP, 1, g, :]))
                chain(nc.vector.tensor_tensor(sq[0:N_CMP], kc[0:N_CMP, g, 0:HD], kc[0:N_CMP, g, 0:HD], ALU.mult))
                chain(nc.vector.tensor_reduce(ms[0:N_CMP, g:g + 1], sq[0:N_CMP], AX, ALU.add))
            dve.sem_inc(msum, 1)
            dve.wait_ge(root, 1)
            chain(nc.vector.reciprocal(ms[0:N_CMP], ms[0:N_CMP]))
            for g in range(GROUPS):
                chain(nc.vector.scalar_tensor_tensor(kc[0:N_CMP, g, 0:HD], kc[0:N_CMP, g, 0:HD], ms[0:N_CMP, g:g + 1],
                                                     gain[0:N_CMP], ALU.mult, ALU.mult))
            dve.sem_inc(normed, 1)
            dve.wait_ge(kturn, 1)
            for g in range(GROUPS):
                chain(nc.vector.tensor_copy(kct[0:AUG, g, :], kps[0:AUG, g, :]))


def attention(env, name, z, heads, q_cols, k_cols, v_cols, aug_q, aug_k, shared_q, out_cols, gates=None, cmp=None, fill=None):
    nc = env.nc
    ctx, sb, ps, sem = stage(nc, name)
    nq = 1 if shared_q else 2
    turns = nq + 2
    units = 2 * NT
    with ctx:
        qs = sb("qs", [P, nq, NT, AUG]); ks = sb("ks", [P, 2, NT, AUG])
        vs = sb("vs", [P, 2, NT, HD])
        qt, kt, prob, probt = (env.spare[:, n * 2 * S:(n + 1) * 2 * S].rearrange("p (u s) -> p u s", u=2) for n in range(4))
        nmax = sb("nmax", [P, 2, NT]); rsum = sb("rsum", [P, 2, NT]); wgt = sb("wgt", [P, 3, NT])
        o1 = sb("o1", [P, NT, HD]); o2 = sb("o2", [P, NT, HD])
        if cmp:
            cs = sb("cs", [P, NT, N_CMP]); cmax = sb("cmax", [P, NT]); csum = sb("csum", [P, NT]); ct = sb("ct", [P, S])
        tq = ps("tq", [P, 2, S]); sc = ps("sc", [P, 2, S]); pt = ps("pt", [P, 2, S]); o = ps("o", [P, 2, NT, HD])
        cps = ps("cps", [P, 512])
        (prep, q_turn, q_moved, scored, maxed, exped, turned, moved, summed, o_free, chain_s, act_s, pool_tick, v_ready,
         c_scored, c_sub, c_exp, c_turn, c_moved, c_out) = (sem(n) for n in (
            "prep", "q_turn", "q_moved", "scored", "maxed", "exped", "turned", "moved", "summed", "o_free", "chain",
            "act_chain", "pool_tick", "v_ready", "c_scored", "c_sub", "c_exp", "c_turn", "c_moved", "c_out"))
        zero_set, filled = sem("zero_set"), sem("filled")
        block = ctx.enter_context(nc.Block())
        copies = 2 * (nq + 2)
        zeros = env.spare[:, 8 * S:8 * S + D]
        if fill is not None:
            @block.sync
            def _(sp):
                sp.wait_ge(zero_set, 1)
                n = fill.shape[0] // P
                sp.dma_start(fill.rearrange("(b p) n -> p b n", p=P), zeros.unsqueeze(1).to_broadcast([P, n, D])).then_inc(filled, 16)
                sp.wait_ge(filled, 16)
        ident = env.const("ident")

        @block.gpsimd
        def _(pool):
            if fill is not None:
                nc.gpsimd.memset(zeros, 0.0).then_inc(zero_set, 1)
            with pool.Fori(0, heads) as i:
                pool.wait_ge(q_turn, i * turns + 1)
                pool.sem_inc(pool_tick, 1)
                for u in range(nq):
                    nc.gpsimd.tensor_copy(qs[:, u, :, 0:HD], z[:, :, bass.ds(q_cols(i, u), HD)]).then_inc(prep, 1)
                    nc.gpsimd.tensor_copy(qs[:, u, :, HD:AUG], aug_q(i, u)).then_inc(prep, 1)
                for u in range(2):
                    nc.gpsimd.tensor_copy(ks[:, u, :, 0:HD], z[:, :, bass.ds(k_cols(i, u), HD)]).then_inc(prep, 1)
                    nc.gpsimd.tensor_copy(ks[:, u, :, HD:AUG], aug_k(i, u)).then_inc(prep, 1)
                pool.wait_ge(summed, i * units + 1)
                pool.sem_inc(pool_tick, 1)
                for u in range(2):
                    nc.gpsimd.tensor_copy(vs[:, u], z[:, :, bass.ds(v_cols(i, u), HD)]).then_inc(v_ready, 1)

        @block.tensor
        def _(pe):
            pe.sem_inc(q_turn, 1)
            pe.sem_inc(summed, 1)
            with pe.Fori(0, heads) as i:
                pe.wait_ge(prep, (i + 1) * copies)
                for n in range(turns):
                    src = qs[:, n] if n < nq else ks[:, n - nq]
                    if n >= 2:
                        pe.wait_ge(q_moved, i * turns + n - 1)
                    for t in range(NT):
                        last = nc.tensor.transpose(tq[0:AUG, n % 2, t * P:(t + 1) * P], src[:, t, :], ident)
                    last.then_inc(q_turn, 1)
                pe.wait_ge(q_moved, (i + 1) * turns)

                def score(n):
                    t, u = n // 2, n % 2
                    end = (t + 1) * P
                    nc.tensor.matmul(sc[:, u, 0:end], qt[0:AUG, u % nq, t * P:end], kt[0:AUG, u, 0:end], start=True, stop=False)
                    nc.tensor.matmul(sc[:, u, t * P:end], ident, env.const("causal"), start=False, stop=True).then_inc(scored, 1)

                def turn(n):
                    t, u = n // 2, n % 2
                    pe.wait_ge(exped, i * units + n + 1)
                    for k in range(t + 1):
                        last = nc.tensor.transpose(pt[:, u, k * P:(k + 1) * P], prob[:, u, k * P:(k + 1) * P], ident)
                    last.then_inc(turned, 1)

                def value(n):
                    t, u = n // 2, n % 2
                    pe.wait_ge(moved, i * units + n + 1)
                    for k in range(t + 1):
                        last = nc.tensor.matmul(o[:, u, t, :], probt[:, u, k * P:(k + 1) * P], vs[:, u, k, :],
                                                start=(k == 0), stop=(k == t))
                    last.then_inc(summed, 1)

                score(0)
                score(1)
                pe.wait_ge(o_free, i + 1)
                if cmp:
                    for t in range(NT):
                        last = nc.tensor.matmul(cps[:, t * N_CMP:(t + 1) * N_CMP], qt[0:AUG, 0, t * P:(t + 1) * P],
                                                cmp["kct"][0:AUG, :], start=True, stop=True)
                    last.then_inc(c_scored, 1)
                pe.wait_ge(v_ready, 2 * (i + 1))
                for n in range(units):
                    turn(n)
                    if n + 2 < units:
                        score(n + 2)
                    if n == 2 and cmp:
                        pe.wait_ge(c_exp, i + 1)
                        for t in range(NT):
                            last = nc.tensor.transpose(tq[0:N_CMP, 0, t * P:(t + 1) * P], cs[:, t, :], ident)
                        last.then_inc(c_turn, 1)
                    if n == 5 and cmp:
                        pe.wait_ge(c_moved, i + 1)
                        for t in range(NT):
                            last = nc.tensor.matmul(cps[:, 256 + t * HD:256 + (t + 1) * HD], ct[0:N_CMP, t * P:(t + 1) * P],
                                                    cmp["vc"][0:N_CMP, :], start=True, stop=True)
                        last.then_inc(c_out, 1)
                    if n >= 1:
                        value(n - 1)
                value(units - 1)

        @block.scalar
        def _(act):
            with act.Fori(0, heads) as i:
                for n in range(turns):
                    act.wait_ge(q_turn, i * turns + n + 2)
                    dst = qt[0:AUG, n] if n < nq else kt[0:AUG, n - nq]
                    nc.scalar.activation(dst, tq[0:AUG, n % 2, :], ACT.Copy).then_inc(q_moved, 1)
                for n in range(units):
                    t, u = n // 2, n % 2
                    act.wait_ge(maxed, i * units + n + 1)
                    nc.scalar.activation(prob[:, u, 0:(t + 1) * P], sc[:, u, 0:(t + 1) * P], ACT.Exp, bias=nmax[:, u, t:t + 1],
                                         accum_out=rsum[:, u, t:t + 1]).then_inc(exped, 1)
                    if n == 1 and cmp:
                        act.wait_ge(c_sub, i + 1)
                        nc.scalar.activation(cs[:], cs[:], ACT.Exp).then_inc(c_exp, 1)
                    if n == 4 and cmp:
                        act.wait_ge(c_turn, i + 1)
                        nc.scalar.activation(ct[0:N_CMP, :], tq[0:N_CMP, 0, :], ACT.Copy).then_inc(c_moved, 1)

        @block.vector
        def _(dve):
            chain = Chain(dve, chain_s)
            per = {False: 5, True: 15}[bool(cmp)]
            dve.sem_inc(o_free, 1)
            with dve.Fori(0, heads) as i:
                chain.loop(i, per)

                def maximum(n):
                    t, u = n // 2, n % 2
                    dve.wait_ge(scored, i * units + n + 1)
                    nc.vector.tensor_reduce(nmax[:, u, t:t + 1], sc[:, u, 0:(t + 1) * P], AX, ALU.max, negate=True).then_inc(maxed, 1)

                def move(n):
                    t, u = n // 2, n % 2
                    dve.wait_ge(turned, i * units + n + 1)
                    nc.vector.tensor_copy(probt[:, u, 0:(t + 1) * P], pt[:, u, 0:(t + 1) * P]).then_inc(moved, 1)

                maximum(0)
                maximum(1)
                if cmp:
                    dve.wait_ge(c_scored, i + 1)
                    chain(nc.vector.tensor_tensor(cs[:], cps[:, 0:NT * N_CMP].rearrange("p (t n) -> p t n", t=NT),
                                                  env.const("cmp_mask").rearrange("p (t n) -> p t n", t=NT), ALU.add))
                    chain(nc.vector.tensor_reduce(cmax[:], cs[:], AX, ALU.max))
                    nc.vector.tensor_tensor(cs[:], cs[:], cmax[:].unsqueeze(2).to_broadcast([P, NT, N_CMP]), ALU.subtract).then_inc(c_sub, 1)
                for n in range(units):
                    move(n)
                    if n + 2 < units:
                        maximum(n + 2)
                dve.wait_ge(summed, (i + 1) * units + 1)
                bc = lambda a: a.unsqueeze(2).to_broadcast([P, NT, HD])
                if not cmp:
                    chain(nc.vector.reciprocal(rsum[:], rsum[:]))
                    for u in range(2):
                        chain(nc.vector.tensor_tensor(o1[:] if u == 0 else o2[:], o[:, u], bc(rsum[:, u]), ALU.mult))
                    dve.sem_inc(o_free, 1)
                    for u in range(2):
                        chain(nc.vector.tensor_copy(z[:, :, bass.ds(out_cols(i, u), HD)], o1[:] if u == 0 else o2[:]))
                else:
                    dve.wait_ge(c_out, i + 1)
                    chain(nc.vector.tensor_reduce(csum[:], cs[:], AX, ALU.add))
                    chain(nc.vector.reciprocal(csum[:], csum[:]))
                    chain(nc.vector.reciprocal(rsum[:], rsum[:]))
                    chain(nc.vector.tensor_tensor(csum[:], csum[:], env.const("cmp_any"), ALU.mult))
                    for b, r in enumerate((csum[:], rsum[:, 0], rsum[:, 1])):
                        chain(nc.vector.tensor_tensor(wgt[:, b, :], gates(i, b), r, ALU.mult))
                    chain(nc.vector.tensor_tensor(o1[:], cps[:, 256:512].rearrange("p (t e) -> p t e", t=NT), bc(wgt[:, 0]), ALU.mult))
                    chain(nc.vector.tensor_tensor(o2[:], o[:, 0], bc(wgt[:, 1]), ALU.mult))
                    chain(nc.vector.tensor_tensor(o1[:], o1[:], o2[:], ALU.add))
                    chain(nc.vector.tensor_tensor(o2[:], o[:, 1], bc(wgt[:, 2]), ALU.mult))
                    dve.sem_inc(o_free, 1)
                    chain(nc.vector.tensor_tensor(o1[:], o1[:], o2[:], ALU.add))
                    chain(nc.vector.tensor_copy(z[:, :, bass.ds(out_cols(i, 0), HD)], o1[:]))
                chain.end(heads)


def out_projection(env, z, chunk_cols, ht, w, g_row, prefetch=()):
    nc, d = env.nc, env.d
    ctx, sb, ps, sem = stage(nc, f"out{env.used}")
    with ctx:
        acc = ps("acc", [P, 2, NT, W]) 
        tmp = env.spare[:, 0:NT * W].rearrange("p (t n) -> p t n", t=NT)
        turn, moved_a, moved_v, freed, chain_s = (sem(n) for n in ("turn", "moved_a", "moved_v", "freed", "chain"))
        block = ctx.enter_context(nc.Block())
        base = env.used

        @block.sync
        def _(sp):
            for w_, c0, cols in prefetch:
                env.load(sp, w_, c0, cols)

        @block.tensor
        def _(pe):
            for k in range(KC):
                for t in range(NT):
                    last = nc.tensor.transpose(acc[:, k // 4, k % 4, t * P:(t + 1) * P],
                                               z[:, t, chunk_cols[k]:chunk_cols[k] + P], env.const("ident"))
                last.then_inc(turn, 1)
            pe.wait_ge(moved_a, 4)
            pe.wait_ge(moved_v, 4)
            project(env, pe, acc, ht, [W, W], freed)

        @block.scalar
        def _(act):
            for k in range(0, KC, 2):
                act.wait_ge(turn, k + 1)
                nc.scalar.copy(ht[:, k, :], acc[:, k // 4, k % 4, :]).then_inc(moved_a, 1)

        @block.vector
        def _(dve):
            chain = Chain(dve, chain_s)
            for k in range(1, KC, 2):
                dve.wait_ge(turn, k + 1)
                nc.vector.tensor_copy(ht[:, k, :], acc[:, k // 4, k % 4, :]).then_inc(moved_v, 1)
            for j in range(2):
                dve.wait_ge(env.w_used, base + j + 1)
                cut = env.x[:, :, j * W:(j + 1) * W]
                if g_row is None:
                    chain(nc.vector.tensor_tensor(cut, cut, acc[:, j], ALU.add))
                    continue
                chain(nc.vector.tensor_tensor(tmp[:], acc[:, j], g_row[:, j * W:(j + 1) * W].unsqueeze(1).to_broadcast([P, NT, W]), ALU.mult))
                chain(nc.vector.tensor_tensor(cut, cut, tmp[:], ALU.add))


def nsa_and_moba(env, z, kct, vc, gs, y_dram):
    ck = env.const("aug_k").rearrange("p (t c) -> p t c", c=2)
    cq = env.const("aug_q").rearrange("p (h t c) -> p h t c", h=8, c=2)
    one = lambda a: a.rearrange("p a t c -> p (a t) c")
    for g in range(GROUPS):
        hpg = NSA_HEADS // GROUPS
        attention(env, f"nsa{g}", z, hpg,
                  lambda i, u: (i + g * hpg) * HD,
                  lambda i, u: (C_KS, C_KW)[u] + g * HD,
                  lambda i, u: (C_VS, C_VW)[u] + g * HD,
                  lambda i, u: one(cq[:, bass.ds(i + g * hpg, 1)]), lambda i, u: ck, True,
                  lambda i, u: (i + g * hpg) * HD,
                  gates=lambda i, b: gs[:, :, bass.ds(i * 3 + g * hpg * 3 + b, 1)].rearrange("p t a -> p (t a)"),
                  cmp={"kct": kct[:, g], "vc": vc[:, g]}, fill=y_dram if g == 0 else None)
    attention(env, "moba", z, MOBA_HEADS // 2,
              lambda i, u: C_QM + i * 2 * HD + u * HD,
              lambda i, u: C_KM + i * 2 * HD + u * HD,
              lambda i, u: C_VM + i * 2 * HD + u * HD,
              lambda i, u: one(cq[:, bass.ds(i * 2 + u, 1)]), lambda i, u: ck, False,
              lambda i, u: C_QM + i * 2 * HD + u * HD)


def sigmoid_stage(env, name, out, in_):
    nc = env.nc
    ctx, sb, ps, sem = stage(nc, name)
    with ctx:
        block = ctx.enter_context(nc.Block())

        @block.scalar
        def _(act):
            nc.scalar.activation(out, in_, ACT.Sigmoid)


def first_mixer(env, mod, y_dram):
    nc = env.nc
    with nc.sbuf_tensor("spare1", [P, 8192], F32) as env.spare, nc.sbuf_tensor("gs", [P, NT, 24], F32) as gs, nc.sbuf_tensor("kct", [P, GROUPS, N_CMP], F32) as kct, \
            nc.sbuf_tensor("vc", [P, GROUPS, HD], F32) as vc, nc.sbuf_tensor("z1", [P, NT, IN1], F32) as z:
        with nc.sbuf_tensor("ht1", [P, KC, S], F32) as ht:
            h = env.spare[:, 0:NT * D].rearrange("p (t n) -> p t n", t=NT)
            norm_transpose(env, "norm1", mod[:, D:2 * D], mod[:, 0:D], ht, h=h)
            in_projection(env, ht, z)
        sigmoid_stage(env, "gates", gs[:], z[:, :, C_G:C_G + 24])
        compress(env, z, kct, vc)
        nsa_and_moba(env, z, kct, vc, gs, y_dram)
        with nc.sbuf_tensor("ht1b", [P, KC, S], F32) as ht:
            out_projection(env, z, [0, 128, 256, 384] + [C_QM + 128 * k for k in range(4)], ht, env.d["w_out"],
                           mod[:, 2 * D:3 * D])


def route(env, ht, gate, dest, slots, expert, n_blocks, row_pick, slot_dram):
    nc, d = env.nc, env.d
    ctx, sb, ps, sem = stage(nc, "route")
    NB = MAX_BLOCKS + 1
    with ctx:
        rw = sb("rw", [P, KC, N_EXP]); rb = sb("rb", [P, N_EXP])
        lg = sb("lg", [P, NT, N_EXP]); top = sb("top", [P, NT, 8]); idx = sb("idx", [P, NT, 8], U32)
        idxf = sb("idxf", [P, NT, 8]); one = sb("one", [P, NT, TOP_K, N_EXP]); chosen = sb("chosen", [P, NT, N_EXP])
        gs = sb("gs", [P, NT]); cnt = sb("cnt", [P, N_EXP]); nb = sb("nb", [P, N_EXP]); tmp = sb("tmp", [P, N_EXP])
        zero = sb("zero", [P, 64], I32); bend = sb("bend", [P, N_EXP]); base = sb("base", [P, N_EXP])
        place = sb("place", [P, TOP_K, N_EXP]); destf = sb("destf", [P, NT * TOP_K]); blk = sb("blk", [P, NT * TOP_K], U32)
        slot = sb("slot", [P, NT * TOP_K], U32); blkf = sb("blkf", [P, NT * TOP_K]); slotf = sb("slotf", [P, NT * TOP_K])
        cell = sb("cell", [P, NT * TOP_K], U32); tok = sb("tok", [P, NT], I32)
        before = sb("before", [P, NB, N_EXP]); ebf = sb("ebf", [P, NB])
        lps = ps("lps", [P, NT, N_EXP]); rps = ps("rps", [P, NT, N_EXP]); cps = ps("cps", [P, N_EXP])
        landed, logits, subbed, exped, picked, ranked, cleared, zeroed, celled, scattered, loaded, chain_s = (sem(n) for n in (
            "landed", "logits", "subbed", "exped", "picked", "ranked", "cleared", "zeroed", "celled", "scattered", "loaded", "chain"))
        block = ctx.enter_context(nc.Block())
        iota = env.const("iota")

        @block.sync
        def _(sp):
            sp.dma_start(rw[:], d["router_w"].rearrange("(k p) n -> p k n", p=P)).then_inc(landed, 16)
            sp.dma_start(rb[:], d["router_b"].partition_broadcast(P)).then_inc(landed, 16)
            sp.wait_ge(cleared, 1)
            sp.dma_start(slot_dram.rearrange("(p b) a -> p (b a)", p=P), zero[:, 0:NB]).then_inc(zeroed, 16)
            sp.wait_ge(scattered, 16 * NT * TOP_K)
            sp.dma_start(slots[:], slot_dram.rearrange("(p b) a -> p (b a)", p=P)).then_inc(loaded, 16)
            sp.wait_ge(loaded, 16)

        @block.tensor
        def _(pe):
            pe.wait_ge(landed, 32)
            for t in range(NT):
                for k in range(KC):
                    last = nc.tensor.matmul(lps[:, t, :], ht[:, k, t * P:(t + 1) * P], rw[:, k, :], start=(k == 0), stop=(k == KC - 1))
            last.then_inc(logits, 1)
            pe.wait_ge(picked, 1)
            for t in range(NT):
                for s in range(t):
                    nc.tensor.matmul(rps[:, t, :], env.const("ones"), chosen[:, s, :], start=(s == 0), stop=False)
                nc.tensor.matmul(rps[:, t, :], env.const("cum_excl"), chosen[:, t, :], start=(t == 0), stop=True)
            for t in range(NT):
                last = nc.tensor.matmul(cps[:], env.const("ones"), chosen[:, t, :], start=(t == 0), stop=(t == NT - 1))
            last.then_inc(ranked, 1)

        @block.scalar
        def _(act):
            act.wait_ge(subbed, 1)
            nc.scalar.activation(gate[:], gate[:], ACT.Exp).then_inc(exped, 1)

        @block.gpsimd
        def _(pool):
            pool.wait_ge(zeroed, 16)
            pool.wait_ge(celled, 1)
            for n in range(NT * TOP_K):
                nc.gpsimd.indirect_dma_start(slot_dram, bass.IndirectOffsetOnAxis(cell[:, n:n + 1], 0),
                                             tok[:, n // TOP_K:n // TOP_K + 1], None).then_inc(scattered, 16)
            pool.wait_ge(scattered, 16 * NT * TOP_K)

        @block.vector
        def _(dve):
            chain = Chain(dve, chain_s)
            chain(nc.vector.memset(zero[:], 0))
            dve.sem_inc(cleared, 1)
            dve.wait_ge(logits, 1)
            for t in range(NT):
                chain(nc.vector.tensor_tensor(lg[:, t, :], lps[:, t, :], rb[:], ALU.add))
                chain(nc.vector.max(top[:, t, :], lg[:, t, :]))
                chain(nc.vector.max_index(idx[:, t, :], top[:, t, :], lg[:, t, :]))
            chain(nc.vector.tensor_copy(idxf[:], idx[:]))
            chain(nc.vector.tensor_tensor(gate[:], top[:, :, 0:TOP_K], top[:, :, 0:1].to_broadcast([P, NT, TOP_K]), ALU.subtract))
            dve.sem_inc(subbed, 1)
            for t in range(NT):
                chain(nc.vector.tensor_tensor(one[:, t], idxf[:, t, 0:TOP_K].unsqueeze(2).to_broadcast([P, TOP_K, N_EXP]),
                                              iota[:, 0:N_EXP].unsqueeze(1).to_broadcast([P, TOP_K, N_EXP]), ALU.is_equal))
                chain(nc.vector.tensor_reduce(chosen[:, t, :], one[:, t].rearrange("p k e -> p e k"), AX, ALU.add))
            dve.sem_inc(picked, 1)
            dve.wait_ge(exped, 1)
            chain(nc.vector.tensor_reduce(gs[:], gate[:], AX, ALU.add))
            chain(nc.vector.reciprocal(gs[:], gs[:]))
            chain(nc.vector.tensor_tensor(gate[:], gate[:], gs[:].unsqueeze(2).to_broadcast([P, NT, TOP_K]), ALU.mult))
            dve.wait_ge(ranked, 1)
            chain(nc.vector.tensor_copy(cnt[:], cps[:]))
            chain(nc.vector.tensor_scalar(nb[:], cnt[:], 0.0, None, ALU.is_gt))
            for j in range(1, NT):
                chain(nc.vector.scalar_tensor_tensor(nb[:], cnt[:], float(j * P), nb[:], ALU.is_gt, ALU.add))
            chain(nc.vector.memset(tmp[:], 0.0))
            chain(nc.vector.tensor_tensor_scan(bend[:], nb[:], tmp[:], 0.0, ALU.add, ALU.add))
            chain(nc.vector.tensor_tensor(base[:], bend[:], nb[:], ALU.subtract))
            chain(nc.vector.tensor_scalar(base[:], base[:], float(P), None, ALU.mult))
            for t in range(NT):
                chain(nc.vector.tensor_tensor(tmp[:], rps[:, t, :], base[:], ALU.add))
                chain(nc.vector.tensor_tensor(place[:], one[:, t], tmp[:].unsqueeze(1).to_broadcast([P, TOP_K, N_EXP]), ALU.mult))
                chain(nc.vector.tensor_reduce(destf[:, t * TOP_K:(t + 1) * TOP_K], place[:], AX, ALU.add))
            chain(nc.vector.tensor_copy(dest[:], destf[:]))
            chain(nc.vector.tensor_scalar(blk[:], dest[:], 7, None, ALU.logical_shift_right))
            chain(nc.vector.tensor_scalar(slot[:], dest[:], P - 1, None, ALU.bitwise_and))
            chain(nc.vector.tensor_copy(blkf[:], blk[:]))
            chain(nc.vector.tensor_copy(slotf[:], slot[:]))
            chain(nc.vector.scalar_tensor_tensor(slotf[:], slotf[:], float(NB), blkf[:], ALU.mult, ALU.add))
            chain(nc.vector.tensor_copy(cell[:], slotf[:]))
            chain(nc.vector.tensor_copy(tok[:], env.const("tok")))
            dve.sem_inc(celled, 1)
            chain(nc.vector.tensor_tensor(before[:], bend[:].unsqueeze(1).to_broadcast([P, NB, N_EXP]),
                                          iota[:, 0:NB].unsqueeze(2).to_broadcast([P, NB, N_EXP]), ALU.is_le))
            chain(nc.vector.tensor_reduce(ebf[:], before[:], AX, ALU.add))
            chain(nc.vector.tensor_scalar(ebf[:], ebf[:], float(N_EXP - 1), None, ALU.min))
            chain(nc.vector.tensor_copy(expert[:], ebf[:]))
            chain(nc.vector.tensor_scalar(row_pick[:], ebf[:], env.const("expert_of_row"), None, ALU.is_equal))
            chain(nc.vector.tensor_copy(n_blocks[:], bend[:, N_EXP - 1:N_EXP]))


def split_biases(env, parts):
    nc, d = env.nc, env.d
    ctx, sb, ps, sem = stage(nc, "bias")
    n = 2 * FF + D
    with ctx:
        b = env.ring[0:96, 0:2, :].rearrange("p a b -> p (a b)")[:, 0:n]
        landed, chain_s = sem("landed"), sem("chain")
        block = ctx.enter_context(nc.Block())

        @block.sync
        def _(sp):
            for i in range(3):
                sp.dma_start(b[i * 32:(i + 1) * 32, 0:2 * FF], d["exp_b1"]).then_inc(landed, 16)
                sp.dma_start(b[i * 32:(i + 1) * 32, 2 * FF:n], d["exp_b2"]).then_inc(landed, 16)

        @block.vector
        def _(dve):
            chain = Chain(dve, chain_s)
            dve.wait_ge(landed, 96)
            for i in range(3):
                rows = slice(i * 32, (i + 1) * 32)
                for _ in range(i):
                    chain(nc.vector.tensor_copy(parts[rows], b[rows]))
                    chain(nc.vector.tensor_tensor(b[rows], b[rows], parts[rows], ALU.subtract))
                chain(nc.vector.tensor_copy(parts[rows], b[rows]))


def expert_blocks(env, slots, expert, n_blocks, row_pick, parts, h_dram, y_dram):
    nc, d = env.nc, env.d
    ctx, sb, ps, sem = stage(nc, "moe")
    CH, RAW, SPLIT = 12, 6, 4
    with ctx:
        xg = sb("xg", [P, D]); col = sb("col", [P, 1], U32)
        xt = [sb("xt_hi", [P, KC, P], F32R), sb("xt_lo", [P, KC, P], F32R)]
        glu, lin, sig, hid = (env.ring[:, RAW + n // 2, (n % 2) * FF:(n % 2 + 1) * FF] for n in range(4))
        glu, lin, sig = (a.rearrange("p (a n) -> p a n", a=2) for a in (glu, lin, sig))
        hidt = [sb("hidt_hi", [P, KC, P], F32R), sb("hidt_lo", [P, KC, P], F32R)]
        y = sb("y", [P, D]); pick = sb("pick", [P, P], BF16)
        w_hi = sb("w_hi", [P, SPLIT, 2048], F32R); w_lo = sb("w_lo", [P, SPLIT, 2048], F32R)
        u = ps("u", [P, 4, W]); yp = ps("yp", [P, 2, W]); tp = ps("tp", [P, 2, W])
        w_landed = [sem(f"w_landed{c}") for c in range(RAW)]
        (split_free, hi_done, lo_dve, lo_pool, col_ready, gathered, x_turn, x_hi, x_lo, u_done, glu_done, sig_done, hid_done, h_turn,
         h_hi, h_lo, pick_ready, y_done, y_moved, stored, chain_s, tick) = (sem(n) for n in (
            "split_free", "hi_done", "lo_dve", "lo_pool", "col_ready", "gathered", "x_turn", "x_hi", "x_lo", "u_done", "glu_done", "sig_done",
            "hid_done", "h_turn", "h_hi", "h_lo", "pick_ready", "y_done", "y_moved", "stored", "chain", "tick"))
        block = ctx.enter_context(nc.Block())
        ident = env.const("ident")
        at = lambda b, c: b * CH + c
        by_pool = lambda c: c % 3 == 2

        def wait_split(eng, b, c, ahead=0):
            if by_pool(c):
                eng.wait_ge(lo_pool, b * (CH // 3) + c // 3 + 1 + (RAW - ahead) // 3)
            else:
                eng.wait_ge(lo_dve, b * (CH * 2 // 3) + c - c // 3 + 1 + (RAW - ahead) * 2 // 3)

        @block.sync
        def _(sp):
            def load(b, c, e):
                wait_split(sp, b, c, RAW)
                raw = env.ring[:, c % RAW, :]
                if c < 8:
                    half, k0 = c // 4, c % 4 * 2
                    rows = d["exp_w1"][bass.ds(e * D + k0 * P, 2 * P), :].rearrange("(a p) (g n) -> p a g n", p=P, g=2)
                    for a in range(2):
                        sp.dma_start(raw.rearrange("p (a g n) -> p a g n", a=2, g=2)[:, a], rows[:, a, :, half * W:(half + 1) * W]
                                     ).then_inc(w_landed[c % RAW], 16)
                else:
                    sp.dma_start(raw.rearrange("p (a n) -> p a n", a=2),
                                 d["exp_w2"][bass.ds(e * FF + (c - 8) * 2 * P, 2 * P), :].rearrange("(a p) n -> p a n", p=P)
                                 ).then_inc(w_landed[c % RAW], 32)

            n = sp.value_load(n_blocks[0:1, 0:1], min_val=1, max_val=MAX_BLOCKS)
            e0 = sp.value_load(expert[0:1, 0:1], min_val=0, max_val=N_EXP - 1)
            for c in range(SPLIT):
                load(0, c, e0)
            with sp.Fori(0, MAX_BLOCKS) as b:
                with sp.If(b < n):
                    e = sp.value_load(expert[0:1, bass.ds(b, 1)], min_val=0, max_val=N_EXP - 1)
                    for c in range(SPLIT, CH):
                        load(b, c, e)
                    e1 = sp.value_load(expert[0:1, bass.ds(b + 1, 1)], min_val=0, max_val=N_EXP - 1)
                    for c in range(SPLIT):
                        load(b + 1, c, e1)

        @block.gpsimd
        def _(pool):
            def rest_of_chunk(b, c):
                pool.wait_ge(hi_done, at(b, c) + 1)
                nc.gpsimd.tensor_tensor(w_lo[:, c % SPLIT, :], env.ring[:, c % RAW, :], w_hi[:, c % SPLIT, :].bitcast(F32), ALU.subtract).then_inc(lo_pool, 1)

            def gather(i):
                nc.gpsimd.tensor_copy(col[:], slots[:, bass.ds(i, 1)] if not isinstance(i, int) else slots[:, i:i + 1]).then_inc(col_ready, 1)
                pool.wait_ge(col_ready, i + 1)
                pool.sem_inc(tick, 1)
                nc.gpsimd.indirect_dma_start(xg[:], None, h_dram, bass.IndirectOffsetOnAxis(col[:, 0:1], 0)).then_inc(gathered, 16)

            n = pool.value_load(n_blocks[0:1, 0:1], min_val=1, max_val=MAX_BLOCKS)
            pool.sem_inc(lo_pool, RAW // 3)
            gather(0)
            rest_of_chunk(0, 2)
            with pool.Fori(0, MAX_BLOCKS) as b:
                with pool.If(b < n):
                    pool.wait_ge(x_turn, (b + 1) * 2)
                    pool.sem_inc(tick, 1)
                    pool.wait_ge(gathered, (b + 1) * 16)
                    pool.sem_inc(tick, 1)
                    gather(b + 1)
                    for c in (5, 8, 11):
                        rest_of_chunk(b, c)
                    rest_of_chunk(b + 1, 2)
            pool.wait_ge(gathered, 16)
            pool.wait_ge(x_turn, n * 2 + 2)
            pool.sem_inc(tick, 1)

        @block.tensor
        def _(pe):
            def turn_rows(i):
                pe.wait_ge(gathered, (i + 1) * 16)
                for q in range(2):
                    for j in range(4):
                        last = nc.tensor.transpose(tp[:, q, j * P:(j + 1) * P], xg[:, (4 * q + j) * P:(4 * q + j + 1) * P], ident)
                    last.then_inc(x_turn, 1)

            def turn_hidden(b, half):
                pe.wait_ge(hid_done, b * 2 + half + 1)
                for j in range(4):
                    last = nc.tensor.transpose(tp[:, half, j * P:(j + 1) * P], hid[:, (4 * half + j) * P:(4 * half + j + 1) * P], ident)
                last.then_inc(h_turn, 1)

            def products(banks, lhs, k, slot, col0, start):
                for l, w in ((0, w_hi), (0, w_lo), (1, w_hi)):
                    for q, bank in enumerate(banks):
                        last = nc.tensor.matmul(bank, lhs[l][:, k, :], w[:, slot, col0 + q * W:col0 + (q + 1) * W],
                                                start=start and l == 0 and w is w_hi, stop=False)
                return last

            pe.sem_inc(split_free, SPLIT)
            pe.sem_inc(y_done, 1)
            n = pe.value_load(n_blocks[0:1, 0:1], min_val=1, max_val=MAX_BLOCKS)
            turn_rows(0)
            with pe.Fori(0, MAX_BLOCKS) as b:
                with pe.If(b < n):
                    pe.wait_ge(x_lo, (b + 1) * 2)
                    for c in range(8):
                        half = c // 4
                        wait_split(pe, b, c)
                        if c == 7:
                            turn_hidden(b, 0)
                        for k in (c % 4 * 2, c % 4 * 2 + 1):
                            last = products([u[:, half, :], u[:, half + 2, :]], xt, k, c % SPLIT, (k % 2) * 2 * W, k == 0)
                        last.then_inc(split_free, 1)
                        if c % 4 == 3:
                            if half == 0:
                                pe.wait_ge(pick_ready, b + 1)
                            for q in (half, half + 2):
                                last = nc.tensor.matmul(u[:, q, :], pick[0:96, :], parts[0:96, q * W:(q + 1) * W], start=False, stop=True)
                            last.then_inc(u_done, 1)
                    pe.wait_ge(y_moved, b + 1)
                    for k in range(KC):
                        c = 8 + k // 2
                        if k % 2 == 0:
                            wait_split(pe, b, c)
                        if k == 3:
                            turn_hidden(b, 1)
                        if k % 4 == 0:
                            pe.wait_ge(h_lo, b * 2 + k // 4 + 1)
                        if k == 6:
                            turn_rows(b + 1)
                        last = products([yp[:, q, :] for q in range(2)], hidt, k, c % SPLIT, (k % 2) * D, k == 0)
                        if k % 2:
                            last.then_inc(split_free, 1)
                    for q in range(2):
                        last = nc.tensor.matmul(yp[:, q, :], pick[0:96, :], parts[0:96, 2 * FF + q * W:2 * FF + (q + 1) * W], start=False, stop=True)
                    last.then_inc(y_done, 1)

        @block.scalar
        def _(act):
            def round_rows(i):
                for q in range(2):
                    act.wait_ge(x_turn, i * 2 + q + 1)
                    nc.scalar.activation(xt[0][:, 4 * q:4 * q + 4, :], tp[:, q, :].rearrange("p (k c) -> p k c", k=4), ACT.Copy).then_inc(x_hi, 1)

            def round_hidden(b, half):
                act.wait_ge(h_turn, b * 2 + half + 1)
                nc.scalar.activation(hidt[0][:, 4 * half:4 * half + 4, :], tp[:, half, :].rearrange("p (k c) -> p k c", k=4), ACT.Copy).then_inc(h_hi, 1)

            def round_chunk(b, c):
                act.wait_ge(w_landed[c % RAW], (b * (CH // RAW) + c // RAW + 1) * 32)
                act.wait_ge(split_free, at(b, c) + 1)
                nc.scalar.activation(w_hi[:, c % SPLIT, :], env.ring[:, c % RAW, :], ACT.Copy).then_inc(hi_done, 1)

            n = act.value_load(n_blocks[0:1, 0:1], min_val=1, max_val=MAX_BLOCKS)
            act.sem_inc(y_moved, 1)
            act.sem_inc(stored, 16)
            for c in range(SPLIT):
                round_chunk(0, c)
            round_rows(0)
            with act.Fori(0, MAX_BLOCKS) as b:
                with act.If(b < n):
                    for c in range(SPLIT, 8):
                        round_chunk(b, c)
                    act.wait_ge(glu_done, b * 2 + 1)
                    nc.scalar.activation(sig[:, 0], glu[:, 0], ACT.Sigmoid, scale=1.702).then_inc(sig_done, 1)
                    round_chunk(b, 8)
                    round_chunk(b, 9)
                    round_hidden(b, 0)
                    round_chunk(b, 10)
                    act.wait_ge(glu_done, b * 2 + 2)
                    nc.scalar.activation(sig[:, 1], glu[:, 1], ACT.Sigmoid, scale=1.702).then_inc(sig_done, 1)
                    round_chunk(b, 11)
                    round_chunk(b + 1, 0)
                    round_hidden(b, 1)
                    round_chunk(b + 1, 1)
                    round_chunk(b + 1, 2)
                    round_rows(b + 1)
                    round_chunk(b + 1, 3)
                    act.wait_ge(y_done, b + 2)
                    act.wait_ge(stored, (b + 1) * 16)
                    nc.scalar.activation(y[:], yp[:].rearrange("p q n -> p (q n)"), ACT.Copy).then_inc(y_moved, 1)
                    act.wait_ge(y_moved, b + 2)
                    act.dma_start(y_dram[bass.ds(b * P, P), :], y[:]).then_inc(stored, 16)
            act.wait_ge(stored, n * 16 + 16)
            act.sem_inc(tick, 1)

        @block.vector
        def _(dve):
            chain = Chain(dve, chain_s)

            def rest_of_rows(i):
                for q in range(2):
                    dve.wait_ge(x_hi, i * 2 + q + 1)
                    cut = slice(4 * q, 4 * q + 4)
                    nc.vector.tensor_tensor(xt[1][:, cut, :], tp[:, q, :].rearrange("p (k c) -> p k c", k=4), xt[0][:, cut, :].bitcast(F32), ALU.subtract).then_inc(x_lo, 1)

            def rest_of_chunk(b, c):
                dve.wait_ge(hi_done, at(b, c) + 1)
                nc.vector.tensor_tensor(w_lo[:, c % SPLIT, :], env.ring[:, c % RAW, :], w_hi[:, c % SPLIT, :].bitcast(F32), ALU.subtract).then_inc(lo_dve, 1)

            def gated(b, half):
                dve.wait_ge(u_done, b * 2 + half + 1)
                nc.vector.tensor_scalar(glu[:, half], u[:, half, :], 7.0, None, ALU.min).then_inc(glu_done, 1)
                chain(nc.vector.tensor_scalar(lin[:, half], u[:, 2 + half, :], 7.0, -7.0, ALU.min, ALU.max))
                dve.wait_ge(glu_done, b * 2 + half + 1)
                chain(nc.vector.scalar_tensor_tensor(lin[:, half], lin[:, half], 1.0, glu[:, half], ALU.add, ALU.mult))
                dve.wait_ge(sig_done, b * 2 + half + 1)
                nc.vector.tensor_tensor(hid[:, half * W:(half + 1) * W], lin[:, half], sig[:, half], ALU.mult).then_inc(hid_done, 1)

            def rest_of_hidden(b, half):
                dve.wait_ge(h_hi, b * 2 + half + 1)
                cut = slice(4 * half, 4 * half + 4)
                nc.vector.tensor_tensor(hidt[1][:, cut, :], tp[:, half, :].rearrange("p (k c) -> p k c", k=4), hidt[0][:, cut, :].bitcast(F32), ALU.subtract).then_inc(h_lo, 1)

            n = dve.value_load(n_blocks[0:1, 0:1], min_val=1, max_val=MAX_BLOCKS)
            dve.sem_inc(lo_dve, RAW * 2 // 3)
            for c in (0, 1, 3):
                rest_of_chunk(0, c)
            rest_of_rows(0)
            with dve.Fori(0, MAX_BLOCKS) as b:
                with dve.If(b < n):
                    chain.loop(b, 4)
                    dve.wait_ge(y_done, b + 1)
                    nc.vector.tensor_scalar(pick[0:96], env.const("ones", 96), row_pick[0:96, bass.ds(b, 1)], None, ALU.mult).then_inc(pick_ready, 1)
                    for c in (4, 6, 7):
                        rest_of_chunk(b, c)
                    gated(b, 0)
                    rest_of_chunk(b, 9)
                    rest_of_hidden(b, 0)
                    rest_of_chunk(b, 10)
                    gated(b, 1)
                    rest_of_chunk(b + 1, 0)
                    rest_of_hidden(b, 1)
                    rest_of_chunk(b + 1, 1)
                    rest_of_rows(b + 1)
                    rest_of_chunk(b + 1, 3)


def combine(env, gate, dest, y_dram, g_row):
    nc = env.nc
    ctx, sb, ps, sem = stage(nc, "comb")
    with ctx:
        acc = sb("acc", [P, D])
        got = [sem(f"got{t}") for t in range(NT)]
        chain_s = sem("chain")
        block = ctx.enter_context(nc.Block())
        row = lambda n: env.ring[:, n // 2, (n % 2) * D:(n % 2 + 1) * D]

        @block.gpsimd
        def _(pool):
            for n in range(NT * TOP_K):
                nc.gpsimd.indirect_dma_start(row(n), None, y_dram, bass.IndirectOffsetOnAxis(dest[:, n:n + 1], 0)).then_inc(got[n // TOP_K], 16)

        @block.vector
        def _(dve):
            chain = Chain(dve, chain_s)
            for t in range(NT):
                dve.wait_ge(got[t], 16 * TOP_K)
                chain(nc.vector.tensor_scalar(acc[:], row(t * TOP_K), gate[:, t, 0:1], None, ALU.mult))
                for k in range(1, TOP_K):
                    chain(nc.vector.scalar_tensor_tensor(acc[:], row(t * TOP_K + k), gate[:, t, k:k + 1], acc[:], ALU.mult, ALU.add))
                chain(nc.vector.tensor_tensor(acc[:], acc[:], g_row, ALU.mult))
                chain(nc.vector.tensor_tensor(env.x[:, t, :], env.x[:, t, :], acc[:], ALU.add))


def first_moe(env, mod, y_dram):
    nc = env.nc
    h_dram = nc.dram_tensor("h_rows", (S, D), F32, kind="Internal").ap()
    slot_dram = nc.dram_tensor("row_tokens", ((MAX_BLOCKS + 1) * P, 1), I32, kind="Internal").ap()
    ctx = ExitStack()
    with ctx:
        sb = lambda n, shape, dt=F32: ctx.enter_context(nc.sbuf_tensor(n, shape, dt))
        gate = sb("gate", [P, NT, TOP_K]); dest = sb("dest", [P, NT * TOP_K], U32)
        slots = sb("slots", [P, MAX_BLOCKS + 1], I32); expert = sb("expert", [P, MAX_BLOCKS + 1], I32)
        n_blocks = sb("n_blocks", [P, 1], I32); row_pick = sb("row_pick", [P, MAX_BLOCKS + 1])
        parts = sb("bias_parts", [P, 2 * FF + D], BF16)
        with nc.sbuf_tensor("ht2", [P, KC, S], F32) as ht:
            norm_transpose(env, "norm2", mod[:, 4 * D:5 * D], mod[:, 3 * D:4 * D], ht, h_dram=h_dram)
            route(env, ht, gate, dest, slots, expert, n_blocks, row_pick, slot_dram)
        split_biases(env, parts)
        expert_blocks(env, slots, expert, n_blocks, row_pick, parts, h_dram, y_dram)
        combine(env, gate, dest, y_dram, mod[:, 5 * D:6 * D])


C2_GATE, C2_Q, C2_F, C2_GA, C2_GB = D, 2 * D, 5 * D, 5 * D + FOX_HEADS, 6 * D + FOX_HEADS
PAD = CONV_W - 1


class Banks:

    def __init__(self, env, acc, done):
        self.env, self.acc, self.done, self.base = env, acc, done, env.used

    def multiply(self, pe, lhs, cols, j, freed, n_freed, parts=KC):
        env, nc = self.env, self.env.nc
        w = env.arrived(pe)
        for t in range(NT):
            if freed is not None:
                pe.wait_ge(freed, n_freed(t))
            for k in range(parts):
                last = nc.tensor.matmul(self.acc[:, t, 0:cols], lhs[:, k, t * P:(t + 1) * P], w[:, k, 0:cols],
                                        start=(k == 0), stop=(k == parts - 1))
            last.then_inc(self.done if t < NT - 1 else env.w_used, 1)

    def ready(self, eng, j, t, first=0):
        if t < NT - 1:
            eng.wait_ge(self.done, (NT - 1) * (j - first) + t + 1)
        else:
            eng.wait_ge(self.env.w_used, self.base + j + 1)


def conv_and_qkv(env, ht, z, conv, glu):
    nc, d = env.nc, env.d
    ctx, sb, ps, sem = stage(nc, "conv")
    with ctx:
        sg = sb("sg", [P, 2, S]); taps = sb("taps", [P, KC, CONV_W]); cols = sb("cols", [P, 3, KC])
        val = ps("val", [P, 2, S]); gat = ps("gat", [P, 2, S]); acc = ps("acc", [P, NT, W])
        landed, val_done, sig_done, glu_done, pad_set, done, freed, chain_s, conv_s = (sem(n) for n in (
            "landed", "val_done", "sig_done", "glu_done", "pad_set", "done", "freed", "chain", "tap"))
        block = ctx.enter_context(nc.Block())
        banks = Banks(env, acc, done)
        banks.base = env.used
        order = [0, C2_GATE, W, C2_GATE + W]
        qkv = [C2_Q + j * W for j in range(3 * D // W)]
        first = len(order)

        @block.sync
        def _(sp):
            sp.dma_start(taps[:], d["conv_w"]).then_inc(landed, 16)
            sp.dma_start(cols[:], d["conv_cols"]).then_inc(landed, 16)
            for c0 in qkv:
                env.load(sp, d["w_in2"], c0, W)

        @block.tensor
        def _(pe):
            for j in range(2):
                wv = env.arrived(pe)
                wg = env.arrived(pe)
                for c in range(4):
                    n = 4 * j + c
                    if n >= 2:
                        pe.wait_ge(glu_done, n - 1)
                    for k in range(KC):
                        last = nc.tensor.matmul(val[:, n % 2, :], wv[:, k, c * P:(c + 1) * P], ht[:, k, :], start=(k == 0), stop=(k == KC - 1))
                    if c == 3:
                        last.then_inc(env.w_used, 1)
                    for k in range(KC):
                        last = nc.tensor.matmul(gat[:, n % 2, :], wg[:, k, c * P:(c + 1) * P], ht[:, k, :], start=(k == 0), stop=(k == KC - 1))
                    last.then_inc(val_done if c < 3 else env.w_used, 1)
            for j in range(len(qkv)):
                banks.multiply(pe, ht, W, j, freed if j else None, lambda t: NT * (j - 1) + t + 1)

        @block.scalar
        def _(act):
            for n in range(KC):
                if n >= 2:
                    act.wait_ge(glu_done, n - 1)
                if n % 4 < 3:
                    act.wait_ge(val_done, n // 4 * 3 + n % 4 + 1)
                else:
                    act.wait_ge(env.w_used, banks.base + (2 if n == 3 else 4))
                nc.scalar.activation(sg[:, n % 2], gat[:, n % 2, :], ACT.Sigmoid).then_inc(sig_done, 1)
            for j in range(len(qkv)):
                for t in range(NT):
                    banks.ready(act, j + first, t, first)
                    nc.scalar.activation(z[:, t, j * W:(j + 1) * W], acc[:, t, :], ACT.Copy,
                                         scale=HD ** -0.5 if j < 2 else 1.0).then_inc(freed, 1)

        @block.vector
        def _(dve):
            chain = Chain(dve, chain_s)
            chain(nc.vector.memset(glu[:, :, 0:PAD], 0.0))
            dve.wait_ge(landed, 32)
            tapped = 0
            for pair in range(KC // 2):
                for u in range(2):
                    n = 2 * pair + u
                    dve.wait_ge(sig_done, n + 1)
                    nc.vector.tensor_tensor(glu[:, u, PAD:PAD + S], val[:, u, :], sg[:, u], ALU.mult).then_inc(glu_done, 1)
                dve.wait_ge(glu_done, 2 * pair + 2)
                for tap in range(CONV_W):
                    for u in range(2):
                        n = 2 * pair + u
                        if tap == 0:
                            ins = nc.vector.tensor_scalar(conv[:, n, :], glu[:, u, 0:S], taps[:, n, 0:1], cols[:, 0, n:n + 1], ALU.mult, ALU.add)
                        else:
                            dve.wait_ge(conv_s, tapped - 1)
                            ins = nc.vector.scalar_tensor_tensor(conv[:, n, :], glu[:, u, tap:tap + S], taps[:, n, tap:tap + 1], conv[:, n, :], ALU.mult, ALU.add)
                        ins.then_inc(conv_s, 1)
                        tapped += 1
                dve.wait_ge(conv_s, tapped)


def conv_norm(env, conv, sq, prefetch):
    nc, d = env.nc, env.d
    ctx, sb, ps, sem = stage(nc, "ln")
    with ctx:
        cols = sb("cols", [P, 3, KC]); mean = sb("mean", [P, S]); rstd = sb("rstd", [P, S]); eps = sb("eps", [P, 1])
        mps = ps("mps", [P, S]); vps = ps("vps", [P, S])
        landed, msum, centred, squared, vsum, root, normed, chain_s = (sem(n) for n in (
            "landed", "msum", "centred", "squared", "vsum", "root", "normed", "chain"))
        block = ctx.enter_context(nc.Block())

        @block.sync
        def _(sp):
            sp.dma_start(cols[:], d["conv_cols"]).then_inc(landed, 16)
            for w, c0, n in prefetch:
                env.load(sp, w, c0, n)

        @block.tensor
        def _(pe):
            for c in range(KC):
                last = nc.tensor.matmul(mps[:], env.const("ones"), conv[:, c, :], start=(c == 0), stop=(c == KC - 1))
            last.then_inc(msum, 1)
            for c in range(KC):
                pe.wait_ge(squared, c + 1)
                last = nc.tensor.matmul(vps[:], env.const("ones"), sq[:, c, :], start=(c == 0), stop=(c == KC - 1))
            last.then_inc(vsum, 1)

        @block.scalar
        def _(act):
            for c in range(KC):
                act.wait_ge(centred, c + 2)
                nc.scalar.activation(sq[:, c, :], conv[:, c, :], ACT.Square).then_inc(squared, 1)
            act.wait_ge(vsum, 1)
            nc.scalar.activation(rstd[:], vps[:], ACT.Sqrt, bias=eps[:], scale=1.0 / D).then_inc(root, 1)
            act.wait_ge(landed, 16)
            for c in range(KC):
                act.wait_ge(normed, c + 1)
                nc.scalar.activation(conv[:, c, :], conv[:, c, :], ACT.Silu, bias=cols[:, 2, c:c + 1], scale=cols[:, 1, c:c + 1])

        @block.vector
        def _(dve):
            chain = Chain(dve, chain_s)
            nc.vector.memset(eps[:], EPS).then_inc(centred, 1)
            dve.wait_ge(msum, 1)
            chain(nc.vector.tensor_scalar(mean[:], mps[:], 1.0 / D, None, ALU.mult))
            for c in range(KC):
                nc.vector.tensor_tensor(conv[:, c, :], conv[:, c, :], mean[:], ALU.subtract).then_inc(centred, 1)
            dve.wait_ge(centred, KC + 1)
            dve.wait_ge(root, 1)
            chain(nc.vector.reciprocal(rstd[:], rstd[:]))
            for c in range(KC):
                nc.vector.tensor_tensor(conv[:, c, :], conv[:, c, :], rstd[:], ALU.mult).then_inc(normed, 1)


def gated_branch(env, name, ht, src, mix, sg, loads, add, prefetch, turn_from=None):
    nc, d = env.nc, env.d
    ctx, sb, ps, sem = stage(nc, name)
    with ctx:
        acc = ps("acc", [P, NT, W]); tp = ps("tp", [P, 2, S])
        done, a_freed, v_freed, sig_done, chain_s, turn, moved = (sem(n) for n in (
            "done", "a_freed", "v_freed", "sig_done", "chain", "turn", "moved"))
        block = ctx.enter_context(nc.Block())
        banks = Banks(env, acc, done)

        @block.sync
        def _(sp):
            for w, c0, n in list(loads) + list(prefetch):
                env.load(sp, w, c0, n)

        @block.tensor
        def _(pe):
            for j in range(4):
                if j == 1 and turn_from is not None:
                    for k in range(KC):
                        if k >= 2:
                            pe.wait_ge(moved, k - 1)
                        for t in range(NT):
                            last = nc.tensor.transpose(tp[:, k % 2, t * P:(t + 1) * P], turn_from[:, t, k * P:(k + 1) * P], env.const("ident"))
                        last.then_inc(turn, 1)
                    pe.wait_ge(moved, KC)
                who = None if j == 0 else (a_freed if j % 2 else v_freed)
                banks.multiply(pe, src if j % 2 else ht, W, j, who, lambda t: (j - 1) // 2 * NT + t + 1)

        @block.scalar
        def _(act):
            for j in (0, 2):
                for t in range(NT):
                    banks.ready(act, j, t)
                    if j:
                        act.wait_ge(v_freed, t + 1)
                    nc.scalar.activation(sg[:, t, :], acc[:, t, :], ACT.Sigmoid).then_inc(a_freed, 1)
                if j == 0 and turn_from is not None:
                    for k in range(KC):
                        act.wait_ge(turn, k + 1)
                        nc.scalar.copy(src[:, k, :], tp[:, k % 2, :]).then_inc(moved, 1)

        @block.vector
        def _(dve):
            for j in (1, 3):
                for t in range(NT):
                    cut = mix[:, t, (j // 2) * W:(j // 2 + 1) * W]
                    banks.ready(dve, j, t)
                    dve.wait_ge(a_freed, (j // 2) * NT + t + 1)
                    if add:
                        nc.vector.tensor_tensor(sg[:, t, :], acc[:, t, :], sg[:, t, :], ALU.mult).then_inc(chain_s, 1)
                        dve.wait_ge(chain_s, (j // 2) * NT + t + 1)
                        nc.vector.tensor_tensor(cut, cut, sg[:, t, :], ALU.add).then_inc(v_freed, 1)
                    else:
                        nc.vector.tensor_tensor(cut, acc[:, t, :], sg[:, t, :], ALU.mult).then_inc(v_freed, 1)


def forget_gates(env, ht, aug_q, aug_k):
    nc, d = env.nc, env.d
    ctx, sb, ps, sem = stage(nc, "forget")
    H = FOX_HEADS
    with ctx:
        wf = sb("wf", [P, KC, H]); bf = sb("bf", [P, H]); f = sb("f", [P, NT, H]); neg = sb("neg", [P, NT, H]); ls = sb("ls", [P, NT, H])
        fps = ps("fps", [P, NT, H]); cps = ps("cps", [P, NT, H])
        landed, logits, mins, exped, plus, logged, lsd, summed, chain_s = (sem(n) for n in (
            "landed", "logits", "mins", "exped", "plus", "logged", "lsd", "summed", "chain"))
        block = ctx.enter_context(nc.Block())

        @block.sync
        def _(sp):
            sp.dma_start(wf[:], d["w_in2"].rearrange("(k p) n -> p k n", p=P)[:, :, C2_F:C2_F + H]).then_inc(landed, 16)
            sp.dma_start(bf[:], d["fox_bf"].partition_broadcast(P)).then_inc(landed, 16)

        @block.tensor
        def _(pe):
            pe.wait_ge(landed, 32)
            for t in range(NT):
                for k in range(KC):
                    last = nc.tensor.matmul(fps[:, t, :], ht[:, k, t * P:(t + 1) * P], wf[:, k, :], start=(k == 0), stop=(k == KC - 1))
            last.then_inc(logits, 1)
            pe.wait_ge(lsd, 1)
            for t in range(NT):
                for s in range(t):
                    nc.tensor.matmul(cps[:, t, :], env.const("ones"), ls[:, s, :], start=(s == 0), stop=False)
                last = nc.tensor.matmul(cps[:, t, :], env.const("cum_incl"), ls[:, t, :], start=(t == 0), stop=True)
            last.then_inc(summed, 1)

        @block.scalar
        def _(act):
            act.wait_ge(mins, 1)
            nc.scalar.activation(ls[:], neg[:], ACT.Exp).then_inc(exped, 1)
            act.wait_ge(plus, 1)
            nc.scalar.activation(ls[:], ls[:], ACT.Ln).then_inc(logged, 1)

        @block.vector
        def _(dve):
            chain = Chain(dve, chain_s)
            dve.wait_ge(logits, 1)
            chain(nc.vector.tensor_tensor(f[:], fps[:], bf[:].unsqueeze(1).to_broadcast([P, NT, H]), ALU.add))
            chain(nc.vector.tensor_scalar(neg[:], f[:], -1.0, None, ALU.mult))
            chain(nc.vector.tensor_tensor(neg[:], neg[:], f[:], ALU.min))
            dve.sem_inc(mins, 1)
            dve.wait_ge(exped, 1)
            chain(nc.vector.tensor_scalar(ls[:], ls[:], 1.0, None, ALU.add))
            dve.sem_inc(plus, 1)
            dve.wait_ge(logged, 1)
            chain(nc.vector.tensor_scalar(f[:], f[:], 0.0, None, ALU.min))
            chain(nc.vector.tensor_tensor(ls[:], f[:], ls[:], ALU.subtract))
            dve.sem_inc(lsd, 1)
            chain(nc.vector.memset(aug_q[:], 1.0))
            chain(nc.vector.memset(aug_k[:], 1.0))
            dve.wait_ge(summed, 1)
            by_head = cps[:].rearrange("p t h -> p h t")
            chain(nc.vector.tensor_copy(aug_q[:, :, :, 0], by_head))
            chain(nc.vector.tensor_scalar(aug_k[:, :, :, 1], by_head, -1.0, None, ALU.mult))


def second_mixer(env):
    nc, d = env.nc, env.d
    C = ExitStack()
    with C:
        sb = lambda n, shape, dt=F32: C.enter_context(nc.sbuf_tensor(n, shape, dt))
        ht = sb("ht3", [P, KC, S]); mix = sb("mix", [P, NT, D])
        env.spare = free = sb("spare2", [P, 8192])
        conv = free[:, 0:KC * S].rearrange("p (k s) -> p k s", k=KC)
        norm_transpose(env, "norm3", None, None, ht, h=mix, gain=d["norm1_g"],
                       prefetch=[(d["w_in2"], c, W) for c in (0, C2_GATE, W, C2_GATE + W)])
        z = sb("z2", [P, NT, 3 * D])
        glu = free[:, KC * S:KC * S + 2 * (S + PAD)].rearrange("p (u s) -> p u s", u=2)
        conv_and_qkv(env, ht, z, conv, glu)
        gates_a = [(d["w_in2"], C2_GA, W), (d["w_conv_out"], 0, W), (d["w_in2"], C2_GA + W, W), (d["w_conv_out"], W, W)]
        gates_b = [(d["w_in2"], C2_GB, W), (d["w_fox_out"], 0, W), (d["w_in2"], C2_GB + W, W), (d["w_fox_out"], W, W)]
        conv_norm(env, conv, mix[:].rearrange("p t (a s) -> p (t a) s", s=S), gates_a)
        sg = free[:, KC * S:KC * S + NT * W].rearrange("p (t n) -> p t n", t=NT)
        gated_branch(env, "ya", ht, conv, mix, sg, [], False, gates_b)
        aug_q = sb("fox_q", [P, FOX_HEADS, NT, 2]); aug_k = sb("fox_k", [P, FOX_HEADS, NT, 2])
        forget_gates(env, ht, aug_q, aug_k)
        one = lambda a: a.rearrange("p a t c -> p (a t) c")
        attention(env, "fox", z, FOX_HEADS // 2,
                  lambda i, u: i * 2 * HD + u * HD,
                  lambda i, u: D + i * 2 * HD + u * HD,
                  lambda i, u: 2 * D + i * 2 * HD + u * HD,
                  lambda i, u: one(aug_q[:, bass.ds(i * 2 + u, 1)]), lambda i, u: one(aug_k[:, bass.ds(i * 2 + u, 1)]), False,
                  lambda i, u: i * 2 * HD + u * HD)
        gated_branch(env, "yb", ht, conv, mix, sg, [], True, [(d["w_out2"], 0, W), (d["w_out2"], W, W)], turn_from=z)
        out_projection(env, mix, [k * P for k in range(KC)], ht, d["w_out2"], None,
                       prefetch=[(d["peer_wq"], j * W, W) for j in range(2)])


def peer_scores(env, ht, scores):
    nc, d = env.nc, env.d
    ctx, sb, ps, sem = stage(nc, "peer_s")
    with ctx:
        keys = sb("keys", [P, 2 * PEER_HEADS, PEER_KEYS]); qt = sb("qt", [P, 2, S])
        qps = ps("qps", [P, 2, S]); sps = ps("sps", [P, 2, NT, PEER_KEYS])
        landed, queried, q_moved, scored, s_moved = (sem(n) for n in ("landed", "queried", "q_moved", "scored", "s_moved"))
        block = ctx.enter_context(nc.Block())
        N = 2 * PEER_HEADS

        @block.sync
        def _(sp):
            sp.dma_start(keys[:], d["peer_k"].rearrange("p h c n -> p (h c) n")).then_inc(landed, 16)
            for j in range(2, 4):
                env.load(sp, d["peer_wq"], j * W, W)

        @block.tensor
        def _(pe):
            def score(n):
                pe.wait_ge(q_moved, n + 1)
                if n >= 2:
                    pe.wait_ge(s_moved, n - 1)
                for t in range(NT):
                    last = nc.tensor.matmul(sps[:, n % 2, t, :], qt[:, n % 2, t * P:(t + 1) * P], keys[:, n, :], start=True, stop=True)
                last.then_inc(scored, 1)

            for n in range(N):
                if n % 4 == 0:
                    w = env.arrived(pe)
                for k in range(KC):
                    last = nc.tensor.matmul(qps[:, n % 2, :], w[:, k, (n % 4) * P:(n % 4 + 1) * P], ht[:, k, :], start=(k == 0), stop=(k == KC - 1))
                last.then_inc(queried, 1)
                if n == 0:
                    pe.wait_ge(landed, 16)
                else:
                    score(n - 1)
                if n % 4 == 3:
                    pe.wait_ge(queried, n + 1)
                    pe.sem_inc(env.w_used, 1)
            score(N - 1)

        @block.scalar
        def _(act):
            for n in range(N):
                act.wait_ge(queried, n + 1)
                if n >= 2:
                    act.wait_ge(scored, n - 1)
                nc.scalar.copy(qt[:, n % 2, :], qps[:, n % 2, :]).then_inc(q_moved, 1)

        @block.vector
        def _(dve):
            for n in range(N):
                dve.wait_ge(scored, n + 1)
                nc.vector.tensor_copy(scores[:, :, n, :], sps[:, n % 2]).then_inc(s_moved, 1)


def peer_select(env, scores, ids, gates):
    nc, d = env.nc, env.d
    ctx, sb, ps, sem = stage(nc, "peer_k")
    K, H = PEER_TOPK, PEER_HEADS
    with ctx:
        val = sb("val", [P, 2 * H, K]); idx = sb("idx", [P, 2 * H, K], U32); idxf = sb("idxf", [P, H, 2, K])
        cand = sb("cand", [P, H, K * K]); top = sb("top", [P, H, K]); pos = sb("pos", [P, H, K], U32)
        part = sb("part", [P, 2, H * K], U32); partf = sb("partf", [P, 2, H * K]); pick = sb("pick", [P, H, K, K])
        e = sb("e", [P, 2, H * K]); gsum = sb("gsum", [P, H])
        chain_s, subbed, exped = sem("chain"), sem("subbed"), sem("exped")
        block = ctx.enter_context(nc.Block())

        @block.scalar
        def _(act):
            for t in range(NT):
                act.wait_ge(subbed, t + 1)
                nc.scalar.activation(gates[:, t], gates[:, t], ACT.Exp).then_inc(exped, 1)

        @block.vector
        def _(dve):
            chain = Chain(dve, chain_s)

            def best(rows, vals, inds):
                last = K // 8 - 1
                for r in range(K // 8):
                    part8 = slice(8 * r, 8 * r + 8)
                    for step in ("max", "index", "drop")[:3 if r < last else 2]:
                        for n, row in enumerate(rows):
                            if step == "max":
                                ins = nc.vector.max(vals[n][:, part8], row)
                            elif step == "index":
                                ins = nc.vector.max_index(inds[n][:, part8], vals[n][:, part8], row)
                            else:
                                ins = nc.vector.match_replace(row, vals[n][:, part8], row, -3e38)
                            if n < len(rows) - 1:
                                chain.n += 1
                                ins.then_inc(chain_s, 1)
                            else:
                                chain(ins)

            for t in range(NT):
                best([scores[:, t, n, :] for n in range(2 * H)], [val[:, n, :] for n in range(2 * H)], [idx[:, n, :] for n in range(2 * H)])
                chain(nc.vector.tensor_copy(idxf[:].rearrange("p h c k -> p (h c) k"), idx[:]))
                for h in range(H):
                    ins = nc.vector.tensor_tensor(cand[:, h, :].rearrange("p (i j) -> p i j", i=K),
                                                  val[:, 2 * h, :].unsqueeze(2).to_broadcast([P, K, K]),
                                                  val[:, 2 * h + 1, :].unsqueeze(1).to_broadcast([P, K, K]), ALU.add)
                    chain.n += 1
                    ins.then_inc(chain_s, 1)
                dve.wait_ge(chain_s, chain.n)
                best([cand[:, h, :] for h in range(H)], [top[:, h, :] for h in range(H)], [pos[:, h, :] for h in range(H)])
                g3 = gates[:, t].rearrange("p (h k) -> p h k", h=H)
                chain(nc.vector.tensor_tensor(g3, top[:], top[:, :, 0:1].to_broadcast([P, H, K]), ALU.subtract))
                dve.sem_inc(subbed, 1)
                flat = pos[:].rearrange("p h k -> p (h k)")
                chain(nc.vector.tensor_scalar(part[:, 0], flat, 4, None, ALU.logical_shift_right))
                chain(nc.vector.tensor_scalar(part[:, 1], flat, K - 1, None, ALU.bitwise_and))
                chain(nc.vector.tensor_copy(partf[:], part[:]))
                for c in range(2):
                    chain(nc.vector.tensor_tensor(pick[:].rearrange("p h k i -> p (h k) i"), partf[:, c].unsqueeze(2).to_broadcast([P, H * K, K]),
                                                  env.const("iota")[:, 0:K].unsqueeze(1).to_broadcast([P, H * K, K]), ALU.is_equal))
                    chain(nc.vector.tensor_tensor(pick[:], pick[:], idxf[:, :, c, :].unsqueeze(2).to_broadcast([P, H, K, K]), ALU.mult))
                    chain(nc.vector.tensor_reduce(e[:, c], pick[:].rearrange("p h k i -> p (h k) i"), AX, ALU.add))
                chain(nc.vector.scalar_tensor_tensor(e[:, 0], e[:, 0], float(PEER_KEYS), e[:, 1], ALU.mult, ALU.add))
                chain(nc.vector.tensor_copy(ids[:, t], e[:, 0]))
                dve.wait_ge(exped, t + 1)
                chain(nc.vector.tensor_reduce(gsum[:], g3, AX, ALU.add))
                chain(nc.vector.reciprocal(gsum[:], gsum[:]))
                chain(nc.vector.tensor_tensor(g3, g3, gsum[:].unsqueeze(2).to_broadcast([P, H, K]), ALU.mult))


def peer_experts(env, h, ids, gates):
    nc, d = env.nc, env.d
    ctx, sb, ps, sem = stage(nc, "peer_x")
    SL, GR = 8, 4
    KS = PEER_HEADS * PEER_TOPK
    STEPS = KS // SL
    with ctx:
        col = sb("col", [P, SL], U32); dot = sb("dot", [P, SL]); act_out = sb("gelu", [P, SL]); diag = sb("diag", [P, SL, P])
        zero = sb("zero", [P, P])
        acc = ps("acc", [P, 2, 2, W])
        gathered = [sem(f"gathered{s}") for s in range(SL)]
        col_ready, v_used, dotted, gelu, coef, t_done, added, zeroed, tick = (sem(n) for n in (
            "col_ready", "v_used", "dotted", "gelu", "coef", "t_done", "added", "zeroed", "tick"))
        block = ctx.enter_context(nc.Block())
        ident = env.const("ident")

        @block.gpsimd
        def _(pool):
            for t in range(NT):
                with pool.Fori(0, STEPS) as i:
                    n0 = i * SL + t * KS
                    for s in range(SL):
                        pool.wait_ge(v_used, n0 + s + 1)
                        pool.sem_inc(tick, 1)
                        nc.gpsimd.tensor_copy(col[:, s:s + 1], ids[:, t, bass.ds(i * SL + s, 1)]).then_inc(col_ready, 1)
                        pool.wait_ge(col_ready, n0 + s + 1)
                        pool.sem_inc(tick, 1)
                        nc.gpsimd.indirect_dma_start(env.ring[:, s, :], None, d["peer_uv"],
                                                     bass.IndirectOffsetOnAxis(col[:, s:s + 1], 0)).then_inc(gathered[s], 16)

        @block.vector
        def _(dve):
            nc.vector.memset(zero[:], 0.0).then_inc(zeroed, 1)
            for t in range(NT):
                with dve.Fori(0, STEPS) as i:
                    n0 = i * SL + t * KS
                    for g in range(SL // GR):
                        for s in range(g * GR, (g + 1) * GR):
                            dve.wait_ge(gathered[s], (i + 1 + t * STEPS) * 16)
                            u = env.ring[:, s, 0:D]
                            nc.vector.tensor_tensor_reduce(u, u, h[:, t, :], 1.0, 0.0, ALU.mult, ALU.add, dot[:, s:s + 1]).then_inc(dotted, 1)
                        for s in range(g * GR, (g + 1) * GR):
                            if s == g * GR:
                                dve.wait_ge(gelu, i * (SL // GR) + g + 1 + t * (KS // GR))
                            nc.vector.tensor_scalar(diag[:, s], ident, act_out[:, s:s + 1], gates[:, t, bass.ds(i * SL + s, 1)],
                                                    ALU.mult, ALU.mult).then_inc(coef, 1)
                dve.wait_ge(t_done, t + 1)
                nc.vector.tensor_tensor(env.x[:, t, :], env.x[:, t, :], acc[:, t % 2].rearrange("p a n -> p (a n)"), ALU.add).then_inc(added, 1)

        @block.scalar
        def _(act):
            for t in range(NT):
                with act.Fori(0, STEPS) as i:
                    for g in range(SL // GR):
                        act.wait_ge(dotted, i * SL + (g + 1) * GR + t * KS)
                        nc.scalar.activation(act_out[:, g * GR:(g + 1) * GR], dot[:, g * GR:(g + 1) * GR], ACT.Gelu_apprx_tanh).then_inc(gelu, 1)

        @block.tensor
        def _(pe):
            pe.sem_inc(v_used, SL)
            pe.wait_ge(zeroed, 1)
            for t in range(NT):
                if t >= 2:
                    pe.wait_ge(added, t - 1)
                for q in range(2):
                    nc.tensor.matmul(acc[:, t % 2, q, :], zero[:], h[:, t, q * W:(q + 1) * W], start=True, stop=False)
                with pe.Fori(0, STEPS) as i:
                    for s in range(SL):
                        pe.wait_ge(coef, i * SL + s + 1 + t * KS)
                        for q in range(2):
                            last = nc.tensor.matmul(acc[:, t % 2, q, :], diag[:, s], env.ring[:, s, D + q * W:D + (q + 1) * W],
                                                    start=False, stop=False)
                        last.then_inc(v_used, 1)
                for q in range(2):
                    last = nc.tensor.matmul(acc[:, t % 2, q, :], zero[:], h[:, t, q * W:(q + 1) * W], start=False, stop=True)
                last.then_inc(t_done, 1)


def final_norm(env):
    nc, d = env.nc, env.d
    ctx, sb, ps, sem = stage(nc, "fin")
    with ctx:
        junk = sb("junk", [P, D]); ms = sb("ms", [P, NT]); eps = sb("eps", [P, 1]); g_row = sb("g_row", [P, D]); y = sb("y", [P, NT, D])
        landed, eps_set, root, act_chain, chain_s, ready, stored = (sem(n) for n in (
            "landed", "eps_set", "root", "act_chain", "chain", "ready", "stored"))
        block = ctx.enter_context(nc.Block())

        @block.sync
        def _(sp):
            sp.dma_start(g_row[:], d["normf_g"].partition_broadcast(P)).then_inc(landed, 16)
            for t in range(NT):
                sp.wait_ge(ready, t + 1)
                sp.dma_start(d["out"][t * P:(t + 1) * P, :], y[:, t, :]).then_inc(stored, 16)
            sp.wait_ge(stored, 16 * NT)

        @block.scalar
        def _(act):
            chain = Chain(act, act_chain)
            for t in range(NT):
                chain(nc.scalar.activation(junk[:], env.x[:, t, :], ACT.Square, accum_out=ms[:, t:t + 1]))
            act.wait_ge(eps_set, 1)
            nc.scalar.activation(ms[:], ms[:], ACT.Sqrt, bias=eps[:], scale=1.0 / D).then_inc(root, 1)

        @block.vector
        def _(dve):
            chain = Chain(dve, chain_s)
            nc.vector.memset(eps[:], EPS).then_inc(eps_set, 1)
            dve.wait_ge(root, 1)
            chain(nc.vector.reciprocal(ms[:], ms[:]))
            dve.wait_ge(landed, 16)
            for t in range(NT):
                nc.vector.scalar_tensor_tensor(y[:, t, :], env.x[:, t, :], ms[:, t:t + 1], g_row[:], ALU.mult, ALU.mult).then_inc(ready, 1)


def second_peer(env):
    nc, d = env.nc, env.d
    C = ExitStack()
    with C:
        sb = lambda n, shape, dt=F32: C.enter_context(nc.sbuf_tensor(n, shape, dt))
        h = sb("h4", [P, NT, D]); ids = sb("ids", [P, NT, P], U32); gates = sb("peer_gates", [P, NT, P])
        scores = sb("scores", [P, NT, 2 * PEER_HEADS, PEER_KEYS])
        with nc.sbuf_tensor("ht4", [P, KC, S], F32) as ht:
            norm_transpose(env, "norm4", None, None, ht, h=h, gain=d["norm2_g"])
            peer_scores(env, ht, scores)
        peer_select(env, scores, ids, gates)
        peer_experts(env, h, ids, gates)
    final_norm(env)


def build(nc, d):
    with ExitStack() as ctx:
        env = Env(nc, ctx, d)
        y_dram = nc.dram_tensor("y_rows", (MAX_BLOCKS * P, D), F32, kind="Internal").ap()
        with nc.sbuf_tensor("mod", [P, 6 * D], F32) as mod:
            modulation(env, mod)
            first_mixer(env, mod, y_dram)
            first_moe(env, mod, y_dram)
        second_mixer(env)
        second_peer(env)


def lay_out(inputs):
    import numpy as np
    g = lambda n: np.ascontiguousarray(inputs[n])
    a = {
        "x": g("x").reshape(S, D),
        "c_col": np.ascontiguousarray(g("c").reshape(KC, P).T),
        "consts": lay_constants(),
        "ada_w": g("ada_w")[0], "ada_b": g("ada_b")[0], "ln1_g": g("ln1_g")[0], "ln2_g": g("ln2_g")[0],
        "w_in": g("w_in")[0], "w_out": g("w_out")[0],
        "cmp_pos": np.ascontiguousarray(g("nsa_cmp_pos")[0].transpose(2, 0, 1).reshape(HD, 2 * CMP_LEN)),
        "cmp_w1": g("nsa_cmp_w1")[0], "cmp_w2": g("nsa_cmp_w2")[0],
        "router_w": g("router_w")[0], "router_b": g("router_b")[0],
        "exp_w1": g("exp_w1")[0].reshape(N_EXP * D, 2 * FF), "exp_b1": g("exp_b1")[0],
        "exp_w2": g("exp_w2")[0].reshape(N_EXP * FF, D), "exp_b2": g("exp_b2")[0],
        "norm1_g": g("norm1_g_2"), "w_in2": g("w_in_2"),
        "conv_w": np.ascontiguousarray(g("conv_w_2").reshape(CONV_W, KC, P).transpose(2, 1, 0)),
        "conv_cols": np.ascontiguousarray(np.stack([g(n).reshape(KC, P).T for n in ("conv_b_2", "conv_ln_g_2", "conv_ln_b_2")], 1)),
        "w_conv_out": g("w_conv_out_2"), "fox_bf": g("fox_bf_2"), "w_fox_out": g("w_fox_out_2"), "w_out2": g("w_out_2"),
        "norm2_g": g("norm2_g_2"), "peer_wq": g("peer_wq_2"),
        "peer_k": np.ascontiguousarray(np.stack([g("peer_k1_2"), g("peer_k2_2")], 1).transpose(3, 0, 1, 2)),
        "peer_uv": np.concatenate([g("peer_u_2"), g("peer_v_2")], 1),
        "normf_g": g("normf_g_2"),
    }
    for n in ("nsa_q_gain", "nsa_k_gain", "moba_q_gain", "moba_k_gain"):
        a[n] = g(n)[0]
    return a


def kernel(**inputs):
    import numpy as _np
    import concourse.bacc as _bacc
    from concourse.bass_utils import run_bass_kernel_spmd as _run

    nc = _bacc.Bacc("TRN2", target_bir_lowering=False, num_devices=1)
    arrays, d = {}, {}
    for name, a in lay_out(inputs).items():
        arrays[f"in_{name}"] = a
        d[name] = nc.dram_tensor(f"in_{name}", a.shape, mybir.dt.from_np(a.dtype), kind="ExternalInput").ap()
    d["out"] = nc.dram_tensor("out", (S, D), F32, kind="ExternalOutput").ap()
    build(nc, d)
    r = _run(nc, [arrays], core_ids=[0])
    return r.results[0]["out"].reshape(1, S, D)
```
